# Optimizing a Trainium2 kernel written in Bass

```python
import jax, jax.numpy as jnp
from jax import lax
import numpy as np

D_MODEL = 2048
BATCH = 1
SEQ = 256
DEPTH = 1

CHUNK = 64
RET_WIDTH = D_MODEL // 2
ATT_WIDTH = D_MODEL - RET_WIDTH
RET_HEADS = 8
ATT_HEADS = 8
RET_HEAD_DIM = RET_WIDTH // RET_HEADS
ATT_HEAD_DIM = ATT_WIDTH // ATT_HEADS
MIX_WIDTH = RET_WIDTH + ATT_WIDTH
IN_WIDTH = 4 * RET_WIDTH + 3 * ATT_WIDTH
LEFT_CHUNKS = 8
BAND = (LEFT_CHUNKS + 1) * CHUNK
REL_CLIP = 128
REL_SIZE = (CHUNK - 1) + REL_CLIP + 1
D_FF = 4 * D_MODEL
ROPE_BASE = 10000.0
EPS = 1e-6
GN_EPS = 1e-5

kernel_name = "hymba_retention_chunkattn_sqrelu_block"

def rms_norm(x, g):
    xf = x.astype(jnp.float32)
    y = xf * lax.rsqrt(jnp.mean(xf * xf, axis=-1, keepdims=True) + EPS)
    return (y * g.astype(jnp.float32)).astype(x.dtype)

def rotary(x, pos):
    half = x.shape[-1] // 2
    inv_freq = ROPE_BASE ** (-jnp.arange(half, dtype=jnp.float32) / half)
    ang = pos[:, None] * inv_freq[None, :]
    cos = jnp.cos(ang)[None, :, None, :]
    sin = jnp.sin(ang)[None, :, None, :]
    xf = x.astype(jnp.float32)
    x1, x2 = xf[..., :half], xf[..., half:]
    out = jnp.concatenate([x1 * cos - x2 * sin, x1 * sin + x2 * cos], axis=-1)
    return out.astype(x.dtype)

def retention(q, k, v):
    b, s, h, d = q.shape
    nc = s // CHUNK
    f32 = jnp.float32
    q = q.astype(f32).reshape(b, nc, CHUNK, h, d)
    k = k.astype(f32).reshape(b, nc, CHUNK, h, d) * (d ** -0.5)
    v = v.astype(f32).reshape(b, nc, CHUNK, h, d)
    log_g = jnp.log1p(-jnp.exp2(-(5.0 + jnp.arange(h, dtype=f32))))
    pos = jnp.arange(CHUNK, dtype=f32)
    intra_decay = jnp.exp(log_g[:, None, None] * jnp.abs(pos[:, None] - pos[None, :]))
    scores = jnp.einsum('bnihd,bnjhd->bnhij', q, k) * intra_decay
    intra = jnp.einsum('bnhij,bnjhe->bnihe', scores, v)
    k_dec = jnp.exp(log_g[None, :] * (CHUNK - 1.0 - pos)[:, None])
    contrib = jnp.einsum('bnjhd,bnjhe->nbhde', k * k_dec[:, :, None], v)
    chunk_dec = jnp.exp(log_g * CHUNK)[:, None, None]

    def step(state, c):
        return chunk_dec * state + c, state

    _, prev = lax.scan(step, jnp.zeros_like(contrib[0]), contrib)
    q_dec = jnp.exp(log_g[None, :] * (pos + 1.0)[:, None])
    cross = jnp.einsum('bnihd,nbhde->bnihe', q * q_dec[:, :, None], prev)
    return (intra + cross).reshape(b, s, h, d)

def head_group_norm(y, g):
    b, s, h, d = y.shape
    mu = jnp.mean(y, axis=-1, keepdims=True)
    var = jnp.mean(jnp.square(y - mu), axis=-1, keepdims=True)
    yn = (y - mu) * lax.rsqrt(var + GN_EPS) * g.astype(jnp.float32).reshape(h, d)
    return yn.reshape(b, s, h * d)

def chunk_attention(q, k, v, rel_bias):
    b, s, h, d = q.shape
    nc = s // CHUNK
    q = q.reshape(b, nc, CHUNK, h, d)
    pad = ((0, 0), (LEFT_CHUNKS, 0), (0, 0), (0, 0), (0, 0))
    kp = jnp.pad(k.reshape(b, nc, CHUNK, h, d), pad)
    vp = jnp.pad(v.reshape(b, nc, CHUNK, h, d), pad)
    band_idx = jnp.arange(nc)[:, None] + jnp.arange(LEFT_CHUNKS + 1)[None, :]
    kb = jnp.take(kp, band_idx, axis=1).reshape(b, nc, BAND, h, d)
    vb = jnp.take(vp, band_idx, axis=1).reshape(b, nc, BAND, h, d)
    scores = jnp.einsum('bnihd,bnjhd->bnhij', q, kb,
                        preferred_element_type=jnp.float32) * (d ** -0.5)
    qi = jnp.arange(CHUNK)[:, None]
    kj = jnp.arange(BAND)[None, :]
    rel = jnp.clip(qi + LEFT_CHUNKS * CHUNK - kj, -(CHUNK - 1), REL_CLIP) + (CHUNK - 1)
    bias = rel_bias.astype(jnp.float32)[:, rel]
    valid = (jnp.arange(nc)[:, None] - LEFT_CHUNKS + kj // CHUNK) >= 0
    scores = jnp.where(valid[None, :, None, None, :], scores + bias[None, None], -1e30)
    probs = jax.nn.softmax(scores, axis=-1).astype(v.dtype)
    out = jnp.einsum('bnhij,bnjhd->bnihd', probs, vb)
    return out.reshape(b, s, h * d)

def setup_inputs(seed: int = 0) -> dict:
    key = jax.random.key(seed)
    ks = jax.random.split(key, 12)
    f32 = jnp.float32
    nrm = lambda k, shape, scale: jax.random.normal(k, shape, f32) * scale
    return {
        "x": jax.random.normal(ks[0], (BATCH, SEQ, D_MODEL), f32),
        "norm1_g": 1.0 + nrm(ks[1], (DEPTH, D_MODEL), 0.05),
        "w_in": nrm(ks[2], (DEPTH, D_MODEL, IN_WIDTH), D_MODEL ** -0.5),
        "ret_norm_g": 1.0 + nrm(ks[3], (DEPTH, RET_WIDTH), 0.05),
        "q_norm_g": 1.0 + nrm(ks[4], (DEPTH, ATT_HEAD_DIM), 0.05),
        "k_norm_g": 1.0 + nrm(ks[5], (DEPTH, ATT_HEAD_DIM), 0.05),
        "rel_bias": nrm(ks[6], (DEPTH, ATT_HEADS, REL_SIZE), 0.2),
        "w_out": nrm(ks[7], (DEPTH, MIX_WIDTH, D_MODEL), MIX_WIDTH ** -0.5),
        "norm2_g": 1.0 + nrm(ks[8], (DEPTH, D_MODEL), 0.05),
        "w_ff1": nrm(ks[9], (DEPTH, D_MODEL, D_FF), D_MODEL ** -0.5),
        "w_ff2": nrm(ks[10], (DEPTH, D_FF, D_MODEL), D_FF ** -0.5),
    }

def reference(x, norm1_g, w_in, ret_norm_g, q_norm_g, k_norm_g, rel_bias,
              w_out, norm2_g, w_ff1, w_ff2):
    b, s, _ = x.shape
    pos = jnp.arange(s, dtype=jnp.float32)
    split_at = [RET_WIDTH, 2 * RET_WIDTH, 3 * RET_WIDTH, 4 * RET_WIDTH,
                4 * RET_WIDTH + ATT_WIDTH, 4 * RET_WIDTH + 2 * ATT_WIDTH]
    for layer in range(DEPTH):
        h = rms_norm(x, norm1_g[layer])
        proj = h @ w_in[layer]
        rq, rk, rv, rg, aq, ak, av = jnp.split(proj, split_at, axis=-1)
        rq = rotary(rq.reshape(b, s, RET_HEADS, RET_HEAD_DIM), pos)
        rk = rotary(rk.reshape(b, s, RET_HEADS, RET_HEAD_DIM), pos)
        rv = rv.reshape(b, s, RET_HEADS, RET_HEAD_DIM)
        ret = head_group_norm(retention(rq, rk, rv), ret_norm_g[layer])
        ret = (jax.nn.silu(rg.astype(jnp.float32)) * ret).astype(x.dtype)
        aq = rms_norm(aq.reshape(b, s, ATT_HEADS, ATT_HEAD_DIM), q_norm_g[layer])
        ak = rms_norm(ak.reshape(b, s, ATT_HEADS, ATT_HEAD_DIM), k_norm_g[layer])
        av = av.reshape(b, s, ATT_HEADS, ATT_HEAD_DIM)
        att = chunk_attention(aq, ak, av, rel_bias[layer])
        x = x + jnp.concatenate([ret, att], axis=-1) @ w_out[layer]
        h = rms_norm(x, norm2_g[layer])
        x = x + jnp.square(jax.nn.relu(h @ w_ff1[layer])) @ w_ff2[layer]
    return x


_drawn_inputs = setup_inputs


def setup_inputs(seed=0):
    import zlib

    import numpy as np

    out = dict(_drawn_inputs(seed))
    spreads = {}
    factors = {'ret_norm_g': 2.876, 'q_norm_g': 8.0, 'k_norm_g': 8.0, 'rel_bias': 3.01}
    for name, (base, spread) in spreads.items():
        noise = np.random.default_rng([zlib.crc32(name.encode()), seed]).standard_normal(out[name].shape)
        drawn = base * np.exp(spread * noise) if base else spread * noise
        out[name] = __import__('jax').numpy.asarray(drawn.astype(out[name].dtype))
    for name, factor in factors.items():
        out[name] = (out[name] * factor).astype(out[name].dtype)
    return out
```

```python
from contextlib import ExitStack

import numpy as np

import concourse.bass as bass
from concourse import mybir

P = 128
D_MODEL, SEQ, CHUNK = 2048, 256, 64
HEADS, HD = 8, 128
D_FF = 4 * D_MODEL
REL_CLIP = 128
EPS, GN_EPS = 1e-6, 1e-5
ROPE_BASE = 10000.0
MT = SEQ // P
KT = D_MODEL // P
N_ATT, N_RET, N = 3 * HD, 4 * HD, 512
SLAB_KT = 4
SLABS = KT // SLAB_KT
PIECES = 8
PIECE_KT = KT // PIECES
SLOTS = 4
AHEAD = 2
OUT_GROUPS = D_MODEL // N
FF_ROUNDS = D_FF // D_MODEL
G_OUT = 2 * HEADS
G_FF = G_OUT + OUT_GROUPS
SCORE_COLS = SEQ + P
MIX_ORDER = list(range(HEADS, 2 * HEADS)) + list(range(HEADS))
GV_NORM1, GV_NORM2, GV_RET, GV_Q, GV_K = 0, KT, 2 * KT, 2 * KT + HEADS, 2 * KT + HEADS + 1
GV = GV_K + 1
CONSTS = 4 * 16


def hybrid_block(nc, x, w_att, w_ret, w_out, w_up, w_down, gains, rel_windows, rope_cos, rope_sin, decay, out):
    f32, f32r = mybir.dt.float32, mybir.dt.float32r
    ALU, ACT, AX = mybir.AluOpType, mybir.ActivationFunctionType, mybir.AxisListType

    with ExitStack() as ctx:
        def sb(name, shape, dt=f32):
            return ctx.enter_context(nc.sbuf_tensor(name, shape, dt))

        def sem(name):
            return ctx.enter_context(nc.semaphore(name))

        xs = sb("xs", [P, MT, D_MODEL])
        hT_hi = sb("hT_hi", [P, KT, SEQ], f32r)
        hT_lo = sb("hT_lo", [P, KT, SEQ], f32r)
        zT_hi = sb("zT_hi", [P, KT, SEQ], f32r)
        zT_lo = sb("zT_lo", [P, KT, SEQ], f32r)
        raw = sb("raw", [P, SLABS, SLAB_KT * N])
        w_hi = sb("w_hi", [P, SLOTS, PIECE_KT * N], f32r)
        w_lo = sb("w_lo", [P, SLOTS, PIECE_KT * N], f32r)
        gv = sb("gv", [P, GV])
        gq = sb("gq", [P, 1])
        cosb = sb("cosb", [P, MT, HD])
        sinb = sb("sinb", [P, MT, HD])
        dec = sb("dec", [P, HEADS, SCORE_COLS])
        bias = sb("bias", [P, HEADS, 2 * P])
        ident = sb("ident", [P, P])
        neg_half = sb("neg_half", [P, 4])
        junk = sb("junk", [P, N])
        ss = sb("ss", [P, MT, OUT_GROUPS])
        ms = sb("ms", [P, MT])
        me = sb("me", [P, MT])
        rstd1 = sb("rstd1", [P, MT])
        ss2 = sb("ss2", [P, MT, OUT_GROUPS])
        ms2 = sb("ms2", [P, MT])
        me2 = sb("me2", [P, MT])
        rstd2 = sb("rstd2", [P, MT])
        ap_ = sb("a_proj", [P, MT, N_ATT])
        a_ss = sb("a_ss", [P, 2 * MT])
        a_ms = sb("a_ms", [P, 2 * MT])
        a_rs = sb("a_rs", [P, 2 * MT])
        a_qk = sb("a_qk", [P, MT, 2 * HD])
        a_qT = sb("a_qT", [P, SEQ])
        a_kT = sb("a_kT", [P, SEQ])
        a_s = sb("a_s", [P, SCORE_COLS])
        a_mx = sb("a_mx", [P, MT])
        a_nmx = sb("a_nmx", [P, MT])
        a_e = sb("a_e", [P, SCORE_COLS])
        a_sum = sb("a_sum", [P, MT])
        a_rc = sb("a_rc", [P, MT])
        a_p = sb("a_p", [P, SCORE_COLS])
        a_pT = sb("a_pT", [P, SCORE_COLS])
        rp = sb("r_proj", [P, MT, N_RET])
        r_c = sb("r_c", [P, MT, 2 * HD])
        r_s = sb("r_s", [P, MT, 2 * HD])
        r_qk = sb("r_qk", [P, MT, 2 * HD])
        r_qT = sb("r_qT", [P, SEQ])
        r_kT = sb("r_kT", [P, SEQ])
        r_sT = sb("r_sT", [P, SCORE_COLS])
        r_st = sb("r_st", [P, MT, 6])
        r_mv = sb("r_mv", [P, MT, 2])
        r_ve = sb("r_ve", [P, MT])
        r_rs = sb("r_rs", [P, MT])
        r_eg = sb("r_eg", [P, MT, HD])
        r_eg1 = sb("r_eg1", [P, MT, HD])
        r_sg = sb("r_sg", [P, MT, HD])
        r_gate = sb("r_gate", [P, MT, HD])
        r_z = sb("r_z", [P, MT, HD])
        r_zn = sb("r_zn", [P, MT, HD])
        u = rp
        hid = sb("hid", [P, MT, N])

        acc = [[ctx.enter_context(nc.psum_tensor(f"acc{p}{m}", [P, N], f32)) for m in range(MT)] for p in range(2)]
        bankA, bankB, bankC, bankD = [ctx.enter_context(nc.psum_tensor(f"bank{b}", [P, N], f32)) for b in "ABCD"]

        x_in = [sem(f"x_in{c}") for c in range(OUT_GROUPS)]
        consts_in = sem("consts_in")
        bias_in = sem("bias_in")
        slab_in = [sem(f"slab_in{s}") for s in range(SLABS)]
        hi_done = sem("hi_done")
        lo_done = sem("lo_done")
        piece_used = sem("piece_used")
        m0_done = sem("m0_done")
        acc_read_act = sem("acc_read_act")
        acc_read_dve = sem("acc_read_dve")
        zeroed = sem("zeroed")
        ident_ok = sem("ident_ok")
        half_ok = sem("half_ok")
        gq_ok = sem("gq_ok")
        mask_ok = sem("mask_ok")
        squared = sem("squared")
        ms_ok = sem("ms_ok")
        me_ok = sem("me_ok")
        rstd1_ok = sem("rstd1_ok")
        tr_done = sem("tr_done")
        tr_hi = sem("tr_hi")
        tr_lo = sem("tr_lo")
        ms2_ok = sem("ms2_ok")
        me2_ok = sem("me2_ok")
        rstd2_ok = sem("rstd2_ok")
        a_ss_ok = sem("a_ss_ok")
        a_ms_ok = sem("a_ms_ok")
        a_rs_ok = sem("a_rs_ok")
        a_qk_ok = sem("a_qk_ok")
        a_T = sem("a_T")
        a_qT_ok = sem("a_qT_ok")
        a_kT_ok = sem("a_kT_ok")
        a_scores = sem("a_scores")
        a_s_ok = sem("a_s_ok")
        a_mx_ok = sem("a_mx_ok")
        a_nmx_ok = sem("a_nmx_ok")
        a_exp_ok = sem("a_exp_ok")
        a_rc_ok = sem("a_rc_ok")
        a_p_ok = sem("a_p_ok")
        a_PT = sem("a_PT")
        a_pT_ok = sem("a_pT_ok")
        a_pv = sem("a_pv")
        a_mix_hi = sem("a_mix_hi")
        a_mix_lo = sem("a_mix_lo")
        r_cs_ok = sem("r_cs_ok")
        r_qk_ok = sem("r_qk_ok")
        r_T = sem("r_T")
        r_qT_ok = sem("r_qT_ok")
        r_kT_ok = sem("r_kT_ok")
        r_scores = sem("r_scores")
        r_sT_ok = sem("r_sT_ok")
        r_y = sem("r_y")
        r_st_ok = sem("r_st_ok")
        r_mv_ok = sem("r_mv_ok")
        r_ve_ok = sem("r_ve_ok")
        r_rs_ok = sem("r_rs_ok")
        r_eg_ok = sem("r_eg_ok")
        r_eg1_ok = sem("r_eg1_ok")
        r_sg_ok = sem("r_sg_ok")
        r_gate_ok = sem("r_gate_ok")
        r_z_ok = sem("r_z_ok")
        r_zn_ok = sem("r_zn_ok")
        r_ZT = sem("r_ZT")
        r_mix_hi = sem("r_mix_hi")
        r_mix_lo = sem("r_mix_lo")
        hid_ok = sem("hid_ok")
        stored = sem("stored")

        def piece_cols(n):
            return PIECE_KT * n

        def tile_cols(m):
            return slice(m * P, (m + 1) * P)

        block = ctx.enter_context(nc.Block())

        @block.sync
        def _(sp):
            def load_slab(g, s, src, n):
                if not isinstance(g, int) or g > 0:
                    sp.wait_ge(lo_done, 8 * g - 8 + 2 * s + 2)
                sp.dma_start(raw[:, s, 0:SLAB_KT * n], src).then_inc(slab_in[s], 16)

            def load_group(g, table, index, n):
                for s in range(SLABS):
                    load_slab(g, s, table[bass.ds(index * (SLABS * P) + s * P, P), :], n)

            x_rows = x.rearrange("b (m p) d -> p (b m) d", p=P)
            for c in range(OUT_GROUPS):
                sp.dma_start(xs[:, :, c * N:(c + 1) * N], x_rows[:, :, c * N:(c + 1) * N]).then_inc(x_in[c], 16)
                if c == 0:
                    sp.dma_start(gv[:], gains).then_inc(consts_in, 16)
                    load_slab(0, 0, w_att[0:P, :], N_ATT)
            for s in range(1, SLABS):
                load_slab(0, s, w_att[s * P:(s + 1) * P, :], N_ATT)
            sp.dma_start(cosb[:], rope_cos.rearrange("(m p) d -> p m d", p=P)).then_inc(consts_in, 16)
            sp.dma_start(sinb[:], rope_sin.rearrange("(m p) d -> p m d", p=P)).then_inc(consts_in, 16)
            sp.dma_start(bias[:], rel_windows).then_inc(bias_in, 16)
            sp.dma_start(dec[:], decay).then_inc(consts_in, 16)
            with sp.Fori(0, HEADS - 1) as i:
                load_group(2 * i + 1, w_ret, i, N_RET)
                load_group(2 * i + 2, w_att, i + 1, N_ATT)
            load_group(2 * HEADS - 1, w_ret, HEADS - 1, N_RET)
            with sp.Fori(0, OUT_GROUPS) as c:
                load_group(G_OUT + c, w_out, c, N)
            with sp.Fori(0, FF_ROUNDS) as g:
                for c in range(4):
                    load_group(G_FF + 8 * g + c, w_up, 4 * g + c, N)
                for c in range(4):
                    load_group(G_FF + 8 * g + 4 + c, w_down, 4 * g + c, N)
            out_rows = out.rearrange("b (m p) d -> p (b m) d", p=P)
            for c in range(4):
                sp.wait_ge(acc_read_dve, 2 * (OUT_GROUPS + 4 * (FF_ROUNDS - 1) + c + 1))
                sp.dma_start(out_rows[:, :, c * N:(c + 1) * N], xs[:, :, c * N:(c + 1) * N]).then_inc(stored, 16)
            sp.wait_ge(stored, 4 * 16)

        @block.gpsimd
        def _(pool):
            nc.gpsimd.memset(neg_half[:], -0.5).then_inc(half_ok, 1)
            nc.gpsimd.memset(ident[:], 0.0).then_inc(zeroed, 1)
            pool.wait_ge(zeroed, 1)
            nc.gpsimd.affine_select(out=ident[:], in_=ident[:], compare_op=ALU.not_equal, fill=1.0, base=0,
                                    pattern=[[-1, P]], channel_multiplier=1).then_inc(ident_ok, 1)
            pool.wait_ge(half_ok, 1)
            pool.wait_ge(me_ok, 1)
            nc.gpsimd.tensor_tensor(rstd1[:], me[:], neg_half[:, 0:MT], ALU.pow).then_inc(rstd1_ok, 1)
            pool.wait_ge(bias_in, 16)
            nc.gpsimd.memset(bias[0:CHUNK, :, P + CHUNK:2 * P], -1e30).then_inc(mask_ok, 1)

            def att_power(h):
                pool.wait_ge(a_ms_ok, h + 1)
                nc.gpsimd.tensor_tensor(a_rs[:], a_ms[:], neg_half[:], ALU.pow).then_inc(a_rs_ok, 1)

            def ret_power(h):
                pool.wait_ge(r_ve_ok, h + 1)
                nc.gpsimd.tensor_tensor(r_rs[:], r_ve[:], neg_half[:, 0:MT], ALU.pow).then_inc(r_rs_ok, 1)

            with pool.Fori(0, HEADS) as h:
                att_power(h)
                ret_power(h)
            pool.wait_ge(me2_ok, 1)
            nc.gpsimd.tensor_tensor(rstd2[:], me2[:], neg_half[:, 0:MT], ALU.pow).then_inc(rstd2_ok, 1)

        X_PAIRS = KT // 2

        @block.tensor
        def _(pe):
            def group(g, par, hi, lo, order, n, acc_free, work):
                for j in range(PIECES):
                    pe.wait_ge(lo_done, 8 * g + j + 1)
                    for m in range(MT):
                        if j == 0:
                            acc_free(m)
                        for t in range(PIECE_KT):
                            k = order[PIECE_KT * j + t]
                            first, last = (j == 0 and t == 0), (j == PIECES - 1 and t == PIECE_KT - 1)
                            wh = w_hi[:, j % SLOTS, t * n:(t + 1) * n]
                            wl = w_lo[:, j % SLOTS, t * n:(t + 1) * n]
                            o = acc[par][m][:, 0:n]
                            nc.tensor.matmul(o, hi[:, k, tile_cols(m)], wh, start=first, stop=False)
                            nc.tensor.matmul(o, hi[:, k, tile_cols(m)], wl, start=False, stop=False)
                            mm = nc.tensor.matmul(o, lo[:, k, tile_cols(m)], wh, start=False, stop=last)
                        if j == PIECES - 1 and m == 0:
                            mm.then_inc(m0_done, 1)
                    mm.then_inc(piece_used, 1)
                    for f in work.get(j, ()):
                        f()

            def free_by_act(groups):
                return lambda m: pe.wait_ge(acc_read_act, 2 * groups + m + 1)

            def free_by_dve(groups):
                return lambda m: pe.wait_ge(acc_read_dve, 2 * groups + m + 1)

            def unused(m):
                pass

            def transpose_pair(e, src, ready):
                ready()
                if not isinstance(e, int) or e >= 2:
                    pe.wait_ge(tr_lo, e - 1)
                bank = bankB if EVEN[0] else bankA
                EVEN[0] = not EVEN[0]
                for t in range(2):
                    for m in range(MT):
                        mm = nc.tensor.transpose(bank[:, (2 * t + m) * P:(2 * t + m + 1) * P],
                                                 src(m)[:, t * P:(t + 1) * P], ident[:])
                mm.then_inc(tr_done, 1)

            def att_T(h):
                pe.wait_ge(a_qk_ok, h + 1)
                for m in range(MT):
                    nc.tensor.transpose(bankA[:, tile_cols(m)], a_qk[:, m, 0:HD], ident[:])
                for m in range(MT):
                    mm = nc.tensor.transpose(bankB[:, tile_cols(m)], a_qk[:, m, HD:2 * HD], ident[:])
                mm.then_inc(a_T, 1)

            def att_scores(h):
                pe.wait_ge(a_qT_ok, h + 1)
                pe.wait_ge(a_kT_ok, h + 1)
                nc.tensor.matmul(bankC[:, 0:P], a_qT[:, 0:P], a_kT[:, 0:P], start=True, stop=True)
                nc.tensor.matmul(bankC[:, P:P + SEQ], a_qT[:, P:SEQ], a_kT[:, 0:SEQ],
                                 start=True, stop=True).then_inc(a_scores, 1)

            def att_PT(h):
                pe.wait_ge(a_p_ok, h + 1)
                for b in range(3):
                    mm = nc.tensor.transpose(bankD[:, b * P:(b + 1) * P], a_p[:, b * P:(b + 1) * P], ident[:])
                mm.then_inc(a_PT, 1)

            def att_pv(h):
                pe.wait_ge(a_pT_ok, h + 1)
                nc.tensor.matmul(bankC[:, 0:SEQ], ap_[:, 0, 2 * HD:3 * HD], a_pT[:, 0:SEQ], start=True, stop=False)
                nc.tensor.matmul(bankC[:, P:SEQ], ap_[:, 1, 2 * HD:3 * HD], a_pT[:, SEQ:SEQ + P],
                                 start=False, stop=True).then_inc(a_pv, 1)

            def ret_T(h):
                pe.wait_ge(r_qk_ok, h + 1)
                for m in range(MT):
                    nc.tensor.transpose(bankA[:, tile_cols(m)], r_qk[:, m, 0:HD], ident[:])
                for m in range(MT):
                    mm = nc.tensor.transpose(bankB[:, tile_cols(m)], r_qk[:, m, HD:2 * HD], ident[:])
                mm.then_inc(r_T, 1)

            def ret_scores(h):
                pe.wait_ge(r_qT_ok, h + 1)
                pe.wait_ge(r_kT_ok, h + 1)
                nc.tensor.matmul(bankD[:, 0:SEQ], r_kT[:, 0:P], r_qT[:, 0:SEQ], start=True, stop=True)
                nc.tensor.matmul(bankD[:, SEQ:SEQ + P], r_kT[:, P:SEQ], r_qT[:, P:SEQ],
                                 start=True, stop=True).then_inc(r_scores, 1)

            def ret_y(h):
                pe.wait_ge(r_sT_ok, h + 1)
                v = [rp[:, m, 2 * HD:3 * HD] for m in range(MT)]
                nc.tensor.matmul(bankC[:, 0:P], r_sT[:, 0:P], v[0], start=True, stop=True)
                nc.tensor.matmul(bankC[:, P:SEQ], r_sT[:, P:SEQ], v[0], start=True, stop=False)
                nc.tensor.matmul(bankC[:, P:SEQ], r_sT[:, SEQ:SEQ + P], v[1], start=False, stop=True).then_inc(r_y, 1)

            def ret_ZT(h):
                pe.wait_ge(r_zn_ok, h + 1)
                for m in range(MT):
                    mm = nc.tensor.transpose(bankA[:, tile_cols(m)], r_zn[:, m, :], ident[:])
                mm.then_inc(r_ZT, 1)

            def att_work(h):
                return {4: [lambda: att_T(h)], 5: [lambda: att_scores(h)], 7: [lambda: att_PT(h)]}

            def ret_work(h):
                return {0: [lambda: att_pv(h)], 3: [lambda: ret_T(h)], 4: [lambda: ret_scores(h)],
                        5: [lambda: ret_y(h)], 7: [lambda: ret_ZT(h)]}

            in_order = list(range(KT))
            EVEN = [False]
            pe.wait_ge(ident_ok, 1)

            def x_pair(e):
                transpose_pair(e, lambda m: xs[:, m, 2 * e * P:2 * (e + 1) * P],
                               lambda: pe.wait_ge(x_in[e // 2], 16))

            for e in range(AHEAD):
                x_pair(e)

            def h_ready(e):
                pe.wait_ge(tr_lo, e + 1)

            work = {j: [lambda e=j + AHEAD: x_pair(e), lambda e=j + 1: h_ready(e)] for j in range(X_PAIRS - AHEAD)}
            work[X_PAIRS - AHEAD] = [lambda: h_ready(X_PAIRS - 1)]
            h_ready(0)
            group(0, 0, hT_hi, hT_lo, in_order, N_ATT, unused, work)
            group(1, 1, hT_hi, hT_lo, in_order, N_RET, unused, att_work(0))
            group(2, 0, hT_hi, hT_lo, in_order, N_ATT, free_by_act(0), ret_work(0))
            with pe.Fori(1, HEADS - 1) as i:
                group(2 * i + 1, 1, hT_hi, hT_lo, in_order, N_RET, free_by_act(2 * i - 1), att_work(i))
                group(2 * i + 2, 0, hT_hi, hT_lo, in_order, N_ATT, free_by_act(2 * i), ret_work(i))
            group(G_OUT - 1, 1, hT_hi, hT_lo, in_order, N_RET, free_by_act(G_OUT - 3), att_work(HEADS - 1))

            work = ret_work(HEADS - 1)
            work = {0: work[0], 1: work[3], 2: work[4], 3: work[5],
                    5: work[7] + [lambda: pe.wait_ge(r_mix_lo, HEADS - 1)],
                    6: [lambda: pe.wait_ge(r_mix_lo, HEADS)]}
            work[1] = work[1] + [lambda: pe.wait_ge(a_mix_lo, HEADS)]

            def stream_pairs(c):
                for b in range(2):
                    transpose_pair(X_PAIRS + 2 * c + b,
                                   lambda m: xs[:, m, c * N + 2 * b * P:c * N + 2 * (b + 1) * P],
                                   lambda: pe.wait_ge(acc_read_dve, 2 * (c + 1)))

            for c in range(OUT_GROUPS):
                free = [free_by_act(G_OUT - 2), free_by_act(G_OUT - 1), free_by_dve(0), free_by_dve(1)][c]
                group(G_OUT + c, c % 2, zT_hi, zT_lo, MIX_ORDER, N, free,
                      work if c == 0 else {1: [lambda: stream_pairs(c - 1)]})
            stream_pairs(OUT_GROUPS - 1)

            def hidden_pairs(g, c):
                for b in range(2):
                    transpose_pair(2 * X_PAIRS + 8 * g + 2 * c + b,
                                   lambda m: hid[:, m, 2 * b * P:2 * (b + 1) * P],
                                   lambda: pe.wait_ge(hid_ok, 2 * (4 * g + c) + 2))

            with pe.Fori(0, FF_ROUNDS) as g:
                up, down = G_FF + 8 * g, G_FF + 8 * g + 4
                acts, dves = G_OUT + 4 * g, OUT_GROUPS + 4 * g
                pe.wait_ge(tr_lo, 2 * X_PAIRS)
                group(up, 0, hT_hi, hT_lo, in_order, N, free_by_dve(dves - 2), {})
                group(up + 1, 1, hT_hi, hT_lo, in_order, N, free_by_dve(dves - 1), {2: [lambda: hidden_pairs(g, 0)]})
                group(up + 2, 0, hT_hi, hT_lo, in_order, N, free_by_act(acts), {2: [lambda: hidden_pairs(g, 1)]})
                group(up + 3, 1, hT_hi, hT_lo, in_order, N, free_by_act(acts + 1), {2: [lambda: hidden_pairs(g, 2)]})
                group(down, 0, zT_hi, zT_lo, in_order, N, free_by_act(acts + 2),
                      {2: [lambda: hidden_pairs(g, 3)],
                       5: [lambda: pe.wait_ge(tr_lo, 2 * X_PAIRS + 8 * g + 8)]})
                group(down + 1, 1, zT_hi, zT_lo, in_order, N, free_by_act(acts + 3), {})
                group(down + 2, 0, zT_hi, zT_lo, in_order, N, free_by_dve(dves), {})
                group(down + 3, 1, zT_hi, zT_lo, in_order, N, free_by_dve(dves + 1), {})

        @block.scalar
        def _(act):
            def hi_piece(g, q, n):
                if q % 2 == 0:
                    act.wait_ge(slab_in[q // 2], 16 * g + 16)
                if not isinstance(g, int) or 8 * g + q >= SLOTS:
                    act.wait_ge(piece_used, 8 * g + q + 1 - SLOTS)
                nc.scalar.activation(w_hi[:, q % SLOTS, 0:PIECE_KT * n],
                                     raw[:, q // 2, (q % 2) * PIECE_KT * n:(q % 2 + 1) * PIECE_KT * n],
                                     ACT.Copy).then_inc(hi_done, 1)

            def group(g, n, n_next, work):
                for j in range(PIECES):
                    if j + AHEAD < PIECES:
                        hi_piece(g, j + AHEAD, n)
                    elif n_next:
                        hi_piece(g + 1, j + AHEAD - PIECES, n_next)
                    for f in work.get(j, ()):
                        f()

            def evacuate(g, par, m, dst, func, scale):
                if m == 0:
                    act.wait_ge(m0_done, g + 1)
                else:
                    act.wait_ge(piece_used, 8 * g + 8)
                n = dst.shape[-1]
                nc.scalar.activation(dst, acc[par][m][:, 0:n], func, scale=scale).then_inc(acc_read_act, 1)

            def att_proj(h):
                for m in range(MT):
                    evacuate(2 * h, 0, m, ap_[:, m, :], ACT.Copy, rstd1[:, m:m + 1])

            def att_squares(h):
                act.wait_ge(acc_read_act, 4 * h + 2)
                for m in range(MT):
                    for s in range(2):
                        i = 2 * m + s
                        ins = nc.scalar.activation(junk[:, i * HD:(i + 1) * HD], ap_[:, m, s * HD:(s + 1) * HD],
                                                   ACT.Square, scale=HD ** -0.5, accum_out=a_ss[:, i:i + 1])
                ins.then_inc(a_ss_ok, 1)

            def att_qT(h):
                act.wait_ge(a_T, h + 1)
                nc.scalar.activation(a_qT[:], bankA[:, 0:SEQ], ACT.Copy, scale=gq[:, 0:1]).then_inc(a_qT_ok, 1)

            def att_exp(h):
                act.wait_ge(a_nmx_ok, h + 1)
                nc.scalar.activation(a_e[:, 0:P], a_s[:, 0:P], ACT.Exp, bias=a_nmx[:, 0:1], accum_out=a_sum[:, 0:1])
                nc.scalar.activation(a_e[:, P:P + SEQ], a_s[:, P:P + SEQ], ACT.Exp, bias=a_nmx[:, 1:2],
                                     accum_out=a_sum[:, 1:2]).then_inc(a_exp_ok, 1)

            def att_pT(h):
                act.wait_ge(a_PT, h + 1)
                nc.scalar.activation(a_pT[:], bankD[:, 0:SCORE_COLS], ACT.Copy).then_inc(a_pT_ok, 1)

            def att_mix(h):
                act.wait_ge(a_pv, h + 1)
                nc.scalar.activation(zT_hi[:, HEADS + h, :], bankC[:, 0:SEQ], ACT.Copy).then_inc(a_mix_hi, 1)

            def ret_proj(h):
                for m in range(MT):
                    evacuate(2 * h + 1, 1, m, rp[:, m, :], ACT.Copy, rstd1[:, m:m + 1])

            def ret_exp(h):
                act.wait_ge(acc_read_act, 4 * h + 4)
                nc.scalar.activation(r_eg[:], rp[:, :, 3 * HD:4 * HD], ACT.Exp, scale=-1.0).then_inc(r_eg_ok, 1)

            def ret_qT(h):
                act.wait_ge(r_T, h + 1)
                nc.scalar.activation(r_qT[:], bankA[:, 0:SEQ], ACT.Copy).then_inc(r_qT_ok, 1)

            def ret_scale(h):
                act.wait_ge(r_z_ok, h + 1)
                act.wait_ge(r_rs_ok, h + 1)
                for m in range(MT):
                    ins = nc.scalar.activation(r_zn[:, m, :], r_z[:, m, :], ACT.Copy, scale=r_rs[:, m:m + 1])
                ins.then_inc(r_zn_ok, 1)

            def ret_mix(h):
                act.wait_ge(r_ZT, h + 1)
                nc.scalar.activation(zT_hi[:, h, :], bankA[:, 0:SEQ], ACT.Copy,
                                     scale=gv[:, bass.ds(h + GV_RET, 1)]).then_inc(r_mix_hi, 1)

            def att_work(h):
                return {0: [lambda: att_proj(h)], 1: [lambda: att_squares(h)], 4: [lambda: att_qT(h)],
                        6: [lambda: att_exp(h)], 7: [lambda: att_pT(h)]}

            def ret_work(h):
                return {0: [lambda: ret_proj(h), lambda: att_mix(h)], 2: [lambda: ret_exp(h)],
                        3: [lambda: ret_qT(h)], 6: [lambda: ret_scale(h)], 7: [lambda: ret_mix(h)]}

            def pair_hi(e, dst_k, gain):
                act.wait_ge(tr_done, e + 1)
                bank = bankB if EVEN[0] else bankA
                EVEN[0] = not EVEN[0]
                dst = zT_hi if gain is None else hT_hi
                if gain is None:
                    nc.scalar.activation(dst[:, dst_k:dst_k + 2, :].rearrange("p k t -> p (k t)"), bank[:],
                                         ACT.Copy).then_inc(tr_hi, 1)
                    return
                for t in range(2):
                    ins = nc.scalar.activation(dst[:, dst_k + t, :], bank[:, t * SEQ:(t + 1) * SEQ], ACT.Copy,
                                               scale=gv[:, gain + dst_k + t:gain + dst_k + t + 1])
                ins.then_inc(tr_hi, 1)

            EVEN = [False]
            act.wait_ge(consts_in, CONSTS)
            pair_hi(0, 0, GV_NORM1)
            hi_piece(0, 0, N_ATT)
            pair_hi(1, 2, GV_NORM1)
            hi_piece(0, 1, N_ATT)
            work = {j: [lambda e=j + AHEAD: pair_hi(e, 2 * e, GV_NORM1)] for j in range(X_PAIRS - AHEAD)}

            def squares(c, sums):
                for m in range(MT):
                    before = MT * (c + (OUT_GROUPS if sums is ss2 else 0)) + m
                    if before:
                        act.wait_ge(squared, before)
                    nc.scalar.activation(junk[:], xs[:, m, c * N:(c + 1) * N], ACT.Square,
                                               scale=D_MODEL ** -0.5, accum_out=sums[:, m, c:c + 1]).then_inc(squared, 1)

            def x_squares():
                for c in range(OUT_GROUPS):
                    act.wait_ge(x_in[c], 16)
                    squares(c, ss)

            work[X_PAIRS - AHEAD] = [x_squares, lambda: act.wait_ge(rstd1_ok, 1)]
            group(0, N_ATT, N_RET, work)
            act.wait_ge(gq_ok, 1)
            with act.Fori(0, HEADS - 1) as i:
                group(2 * i + 1, N_RET, N_ATT, att_work(i))
                group(2 * i + 2, N_ATT, N_RET, ret_work(i))
            group(G_OUT - 1, N_RET, N, att_work(HEADS - 1))

            work = ret_work(HEADS - 1)
            work = {0: work[0] + work[2], 1: work[3], 4: work[6], 5: work[7]}
            group(G_OUT, N, N, work)

            def stream_split(c):
                for b in range(2):
                    pair_hi(X_PAIRS + 2 * c + b, 4 * c + 2 * b, GV_NORM2)
                act.wait_ge(acc_read_dve, 2 * c + 2)
                squares(c, ss2)

            for c in range(1, OUT_GROUPS):
                group(G_OUT + c, N, N if c < OUT_GROUPS - 1 else None, {2: [lambda: stream_split(c - 1)]})
            stream_split(OUT_GROUPS - 1)

            def hidden_relu(g, c):
                act.wait_ge(rstd2_ok, 1)
                for m in range(MT):
                    evacuate(G_FF + 8 * g + c, c % 2, m, u[:, m, :], ACT.Relu, rstd2[:, m:m + 1])

            def hidden_split(g, c):
                for b in range(2):
                    pair_hi(2 * X_PAIRS + 8 * g + 2 * c + b, 4 * c + 2 * b, None)

            with act.Fori(0, FF_ROUNDS) as g:
                for q in range(AHEAD):
                    hi_piece(G_FF + 8 * g, q, N)
                for c in range(8):
                    work = {}
                    if 1 <= c <= 4:
                        work = {0: [lambda: hidden_relu(g, c - 1)], 2: [lambda: hidden_split(g, c - 1)]}
                    group(G_FF + 8 * g + c, N, N if c < 7 else None, work)

        @block.vector
        def _(dve):
            def lo_piece(g, q, n):
                dve.wait_ge(hi_done, 8 * g + q + 1)
                nc.vector.tensor_tensor(w_lo[:, q % SLOTS, 0:PIECE_KT * n],
                                        raw[:, q // 2, (q % 2) * PIECE_KT * n:(q % 2 + 1) * PIECE_KT * n],
                                        w_hi[:, q % SLOTS, 0:PIECE_KT * n].bitcast(f32),
                                        ALU.subtract).then_inc(lo_done, 1)

            def group(g, n, n_next, work):
                for j in range(PIECES):
                    if j + AHEAD < PIECES:
                        lo_piece(g, j + AHEAD, n)
                    elif n_next:
                        lo_piece(g + 1, j + AHEAD - PIECES, n_next)
                    for f in work.get(j, ()):
                        f()

            def att_mean_squares(h):
                dve.wait_ge(a_ss_ok, h + 1)
                nc.vector.tensor_scalar(a_ms[:], a_ss[:], EPS, None, ALU.add).then_inc(a_ms_ok, 1)

            def att_norm(h):
                dve.wait_ge(a_rs_ok, h + 1)
                for m in range(MT):
                    for s in range(2):
                        i = 2 * m + s
                        ins = nc.vector.tensor_scalar(a_qk[:, m, s * HD:(s + 1) * HD], ap_[:, m, s * HD:(s + 1) * HD],
                                                      a_rs[:, i:i + 1], None, ALU.mult)
                ins.then_inc(a_qk_ok, 1)

            def att_kT(h):
                dve.wait_ge(a_T, h + 1)
                nc.vector.tensor_scalar(a_kT[:], bankB[:, 0:SEQ], gv[:, GV_K:GV_K + 1], None,
                                        ALU.mult).then_inc(a_kT_ok, 1)

            def att_bias_max(h):
                dve.wait_ge(a_scores, h + 1)
                hb = bias[:, bass.ds(h, 1), :].rearrange("p a k -> p (a k)")
                nc.vector.tensor_tensor(a_s[:, 0:P], bankC[:, 0:P], hb[:, P:2 * P], ALU.add)
                nc.vector.tensor_tensor(a_s[:, P:P + SEQ], bankC[:, P:P + SEQ], hb, ALU.add).then_inc(a_s_ok, 1)
                dve.wait_ge(a_s_ok, h + 1)
                nc.vector.tensor_reduce(a_mx[:, 0:1], a_s[:, 0:P], AX.X, ALU.max)
                nc.vector.tensor_reduce(a_mx[:, 1:2], a_s[:, P:P + SEQ], AX.X, ALU.max).then_inc(a_mx_ok, 1)
                dve.wait_ge(a_mx_ok, h + 1)
                nc.vector.tensor_scalar(a_nmx[:], a_mx[:], -1.0, None, ALU.mult).then_inc(a_nmx_ok, 1)

            def att_probs(h):
                dve.wait_ge(a_exp_ok, h + 1)
                nc.vector.reciprocal(a_rc[:], a_sum[:]).then_inc(a_rc_ok, 1)
                dve.wait_ge(a_rc_ok, h + 1)
                nc.vector.tensor_scalar(a_p[:, 0:P], a_e[:, 0:P], a_rc[:, 0:1], None, ALU.mult)
                nc.vector.tensor_scalar(a_p[:, P:P + SEQ], a_e[:, P:P + SEQ], a_rc[:, 1:2], None,
                                        ALU.mult).then_inc(a_p_ok, 1)

            def att_mix(h):
                dve.wait_ge(a_mix_hi, h + 1)
                nc.vector.tensor_tensor(zT_lo[:, HEADS + h, :], bankC[:, 0:SEQ],
                                        zT_hi[:, HEADS + h, :].bitcast(f32), ALU.subtract).then_inc(a_mix_lo, 1)

            def ret_rotate(h):
                dve.wait_ge(acc_read_act, 4 * h + 4)
                for m in range(MT):
                    qk = rp[:, m, 0:2 * HD]
                    cos = cosb[:, m, :].rearrange("p (a d) -> p a d", a=1).to_broadcast([P, 2, HD])
                    nc.vector.tensor_tensor(r_c[:, m, :].rearrange("p (s d) -> p s d", s=2),
                                            qk.rearrange("p (s d) -> p s d", s=2), cos, ALU.mult)
                    for half in range(2):
                        src = qk.rearrange("p (s f d) -> p s f d", s=2, f=2)[:, :, 1 - half, :]
                        dst = r_s[:, m, :].rearrange("p (s f d) -> p s f d", s=2, f=2)[:, :, half, :]
                        sin = sinb[:, m, half * HD // 2:(half + 1) * HD // 2].rearrange("p (a d) -> p a d", a=1)
                        ins = nc.vector.tensor_tensor(dst, src, sin.to_broadcast([P, 2, HD // 2]), ALU.mult)
                ins.then_inc(r_cs_ok, 1)

            def ret_rotated(h):
                dve.wait_ge(r_cs_ok, h + 1)
                nc.vector.tensor_tensor(r_qk[:], r_c[:], r_s[:], ALU.add).then_inc(r_qk_ok, 1)

            def ret_kT(h):
                dve.wait_ge(r_T, h + 1)
                nc.vector.tensor_copy(r_kT[:], bankB[:, 0:SEQ]).then_inc(r_kT_ok, 1)

            def ret_sigmoid(h):
                dve.wait_ge(r_eg_ok, h + 1)
                nc.vector.tensor_scalar(r_eg1[:], r_eg[:], 1.0, None, ALU.add).then_inc(r_eg1_ok, 1)
                dve.wait_ge(r_eg1_ok, h + 1)
                nc.vector.reciprocal(r_sg[:], r_eg1[:]).then_inc(r_sg_ok, 1)

            def ret_decay(h):
                dve.wait_ge(r_scores, h + 1)
                nc.vector.tensor_tensor(r_sT[:], bankD[:, 0:SCORE_COLS],
                                        dec[:, bass.ds(h, 1), :].rearrange("p a k -> p (a k)"),
                                        ALU.mult).then_inc(r_sT_ok, 1)

            def ret_norm(h):
                dve.wait_ge(r_y, h + 1)
                for m in range(MT):
                    ins = nc.vector.bn_stats(r_st[:, m, :], bankC[:, tile_cols(m)])
                ins.then_inc(r_st_ok, 1)
                dve.wait_ge(r_sg_ok, h + 1)
                dve.wait_ge(r_st_ok, h + 1)
                nc.vector.tensor_tensor(r_gate[:], rp[:, :, 3 * HD:4 * HD], r_sg[:], ALU.mult).then_inc(r_gate_ok, 1)
                for m in range(MT):
                    ins = nc.vector.bn_aggr(r_mv[:, m, :], r_st[:, m, :])
                ins.then_inc(r_mv_ok, 1)
                dve.wait_ge(r_mv_ok, h + 1)
                nc.vector.tensor_scalar(r_ve[:], r_mv[:, :, 1], GN_EPS, None, ALU.add).then_inc(r_ve_ok, 1)
                dve.wait_ge(r_gate_ok, h + 1)
                for m in range(MT):
                    ins = nc.vector.scalar_tensor_tensor(out=r_z[:, m, :], in0=bankC[:, tile_cols(m)],
                                                         scalar=r_mv[:, m, 0:1], in1=r_gate[:, m, :],
                                                         op0=ALU.subtract, op1=ALU.mult)
                ins.then_inc(r_z_ok, 1)

            def ret_mix(h):
                dve.wait_ge(r_mix_hi, h + 1)
                nc.vector.scalar_tensor_tensor(out=zT_lo[:, h, :], in0=bankA[:, 0:SEQ],
                                               scalar=gv[:, bass.ds(h + GV_RET, 1)],
                                               in1=zT_hi[:, h, :].bitcast(f32),
                                               op0=ALU.mult, op1=ALU.subtract).then_inc(r_mix_lo, 1)

            def att_work(h):
                return {2: [lambda: att_mean_squares(h)], 3: [lambda: att_norm(h)], 4: [lambda: att_kT(h)],
                        5: [lambda: att_bias_max(h)], 6: [lambda: att_probs(h)]}

            def ret_work(h):
                return {0: [lambda: att_mix(h)], 1: [lambda: ret_rotate(h)], 2: [lambda: ret_rotated(h)],
                        3: [lambda: ret_kT(h), lambda: ret_sigmoid(h)], 4: [lambda: ret_decay(h)],
                        5: [lambda: ret_norm(h)], 7: [lambda: ret_mix(h)]}

            def pair_lo(e, dst_k, gain):
                dve.wait_ge(tr_hi, e + 1)
                bank = bankB if EVEN[0] else bankA
                EVEN[0] = not EVEN[0]
                if gain is None:
                    nc.vector.tensor_tensor(zT_lo[:, dst_k:dst_k + 2, :].rearrange("p k t -> p (k t)"), bank[:],
                                            zT_hi[:, dst_k:dst_k + 2, :].rearrange("p k t -> p (k t)").bitcast(f32),
                                            ALU.subtract).then_inc(tr_lo, 1)
                    return
                for t in range(2):
                    ins = nc.vector.scalar_tensor_tensor(out=hT_lo[:, dst_k + t, :], in0=bank[:, t * SEQ:(t + 1) * SEQ],
                                                         scalar=gv[:, gain + dst_k + t:gain + dst_k + t + 1],
                                                         in1=hT_hi[:, dst_k + t, :].bitcast(f32),
                                                         op0=ALU.mult, op1=ALU.subtract)
                ins.then_inc(tr_lo, 1)

            EVEN = [False]
            dve.wait_ge(consts_in, CONSTS)
            nc.vector.tensor_scalar(gq[:], gv[:, GV_Q:GV_Q + 1], HD ** -0.5, None, ALU.mult).then_inc(gq_ok, 1)
            pair_lo(0, 0, GV_NORM1)
            lo_piece(0, 0, N_ATT)
            pair_lo(1, 2, GV_NORM1)
            lo_piece(0, 1, N_ATT)
            work = {j: [lambda e=j + AHEAD: pair_lo(e, 2 * e, GV_NORM1)] for j in range(X_PAIRS - AHEAD)}

            def x_mean_squares():
                dve.wait_ge(squared, MT * OUT_GROUPS)
                nc.vector.tensor_reduce(ms[:], ss[:], AX.X, ALU.add).then_inc(ms_ok, 1)
                dve.wait_ge(ms_ok, 1)
                nc.vector.tensor_scalar(me[:], ms[:], EPS, None, ALU.add).then_inc(me_ok, 1)

            work[X_PAIRS - AHEAD] = [x_mean_squares]
            group(0, N_ATT, N_RET, work)
            dve.wait_ge(mask_ok, 1)
            with dve.Fori(0, HEADS - 1) as i:
                group(2 * i + 1, N_RET, N_ATT, att_work(i))
                group(2 * i + 2, N_ATT, N_RET, ret_work(i))
            group(G_OUT - 1, N_RET, N, att_work(HEADS - 1))
            work = ret_work(HEADS - 1)
            work = {0: work[0] + work[1] + work[2], 1: work[3], 2: work[4], 3: work[5], 5: work[7]}
            group(G_OUT, N, N, work)

            def add_to_stream(g, par, c):
                for m in range(MT):
                    if m == 0:
                        dve.wait_ge(m0_done, g + 1)
                    else:
                        dve.wait_ge(piece_used, 8 * g + 8)
                    cols = xs[:, m, c * N:(c + 1) * N]
                    nc.vector.tensor_tensor(cols, acc[par][m][:], cols, ALU.add).then_inc(acc_read_dve, 1)

            def stream_split(c):
                for b in range(2):
                    pair_lo(X_PAIRS + 2 * c + b, 4 * c + 2 * b, GV_NORM2)

            for c in range(1, OUT_GROUPS):
                group(G_OUT + c, N, N if c < OUT_GROUPS - 1 else None,
                      {0: [lambda: add_to_stream(G_OUT + c - 1, (c - 1) % 2, c - 1)], 2: [lambda: stream_split(c - 1)]})
            add_to_stream(G_FF - 1, 1, OUT_GROUPS - 1)
            stream_split(OUT_GROUPS - 1)
            dve.wait_ge(squared, 2 * MT * OUT_GROUPS)
            nc.vector.tensor_reduce(ms2[:], ss2[:], AX.X, ALU.add).then_inc(ms2_ok, 1)
            dve.wait_ge(ms2_ok, 1)
            nc.vector.tensor_scalar(me2[:], ms2[:], EPS, None, ALU.add).then_inc(me2_ok, 1)

            def hidden_square(g, c):
                dve.wait_ge(acc_read_act, 2 * (G_OUT + 4 * g + c) + 2)
                for m in range(MT):
                    nc.vector.tensor_tensor(hid[:, m, :], u[:, m, :], u[:, m, :], ALU.mult).then_inc(hid_ok, 1)

            def hidden_split(g, c):
                for b in range(2):
                    pair_lo(2 * X_PAIRS + 8 * g + 2 * c + b, 4 * c + 2 * b, None)

            with dve.Fori(0, FF_ROUNDS) as g:
                for q in range(AHEAD):
                    lo_piece(G_FF + 8 * g, q, N)
                for c in range(8):
                    work = {}
                    if 1 <= c <= 4:
                        work = {1: [lambda: hidden_square(g, c - 1)], 2: [lambda: hidden_split(g, c - 1)]}
                    if c >= 5:
                        work = {0: [lambda: add_to_stream(G_FF + 8 * g + c - 1, (c - 1) % 2, c - 5)]}
                    group(G_FF + 8 * g + c, N, N if c < 7 else None, work)
                add_to_stream(G_FF + 8 * g + 7, 1, 3)


def tables():
    f32 = np.float32
    half = HD // 2
    inv_freq = (ROPE_BASE ** (-np.arange(half, dtype=f32) / half)).astype(f32)
    angle = (np.arange(SEQ, dtype=f32)[:, None] * inv_freq[None, :]).astype(f32)
    cos, sin = np.cos(angle).astype(f32), np.sin(angle).astype(f32)
    log_g = np.log1p(-np.exp2(-(5.0 + np.arange(HEADS))))
    key, query = np.arange(SEQ)[:, None], np.arange(SEQ)[None, :]
    full = np.exp(log_g[:, None, None] * np.abs(query - key)) * (key // CHUNK <= query // CHUNK) * HD ** -0.5
    decay = np.concatenate([full[:, 0:P, :], full[:, P:, P:]], axis=2).transpose(1, 0, 2)
    return np.concatenate([cos, cos], 1), np.concatenate([-sin, sin], 1), np.ascontiguousarray(decay, dtype=f32)


def slabs(w, order=range(KT)):
    t = w.reshape(KT, P, -1)[list(order)].reshape(SLABS, SLAB_KT, P, -1)
    return t.transpose(0, 2, 1, 3).reshape(SLABS * P, -1)


def kernel(x, norm1_g, w_in, ret_norm_g, q_norm_g, k_norm_g, rel_bias, w_out, norm2_g, w_ff1, w_ff2):
    import concourse.bacc as bacc
    from concourse.bass_utils import run_bass_kernel_spmd as run

    x = np.asarray(x)
    w = np.asarray(w_in)[0].reshape(D_MODEL, 7, HEADS, HD)
    head = lambda first, last, h: w[:, first:last, h, :].reshape(D_MODEL, -1)
    up, down = np.asarray(w_ff1)[0], np.asarray(w_ff2)[0]
    vectors = [np.asarray(v)[0].reshape(-1, P).T for v in (norm1_g, norm2_g, ret_norm_g, q_norm_g, k_norm_g)]
    rel = np.pad(np.asarray(rel_bias)[0], ((0, 0), (P - CHUNK, P - 1)), mode="edge")[:, ::-1]
    windows = np.lib.stride_tricks.sliding_window_view(rel, 2 * P, axis=1)[:, ::-1].transpose(1, 0, 2)
    cos, sin, decay = tables()
    arrays = {
        "x": x,
        "w_att": np.concatenate([slabs(head(4, 7, h)) for h in range(HEADS)]),
        "w_ret": np.concatenate([slabs(head(0, 4, h)) for h in range(HEADS)]),
        "w_out": np.concatenate([slabs(np.asarray(w_out)[0][:, c * N:(c + 1) * N], MIX_ORDER)
                                 for c in range(OUT_GROUPS)]),
        "w_up": np.concatenate([slabs(up[:, c * N:(c + 1) * N]) for c in range(D_FF // N)]),
        "w_down": np.concatenate([slabs(down[g * D_MODEL:(g + 1) * D_MODEL, c * N:(c + 1) * N])
                                  for g in range(FF_ROUNDS) for c in range(D_MODEL // N)]),
        "gains": np.concatenate(vectors, axis=1),
        "rel_windows": windows,
        "rope_cos": cos,
        "rope_sin": sin,
        "decay": decay,
    }
    nc = bacc.Bacc("TRN2", target_bir_lowering=False, num_devices=1)
    arrays = {f"in_{n}": np.ascontiguousarray(a) for n, a in arrays.items()}
    args = [nc.dram_tensor(n, a.shape, mybir.dt.from_np(a.dtype), kind="ExternalInput").ap()
            for n, a in arrays.items()]
    args.append(nc.dram_tensor("out", x.shape, mybir.dt.from_np(x.dtype), kind="ExternalOutput").ap())
    hybrid_block(nc, *args)
    return run(nc, [arrays], core_ids=[0]).results[0]["out"]
```

```python
from contextlib import ExitStack

import numpy as np

import concourse.bass as bass
from concourse import mybir

P = 128
D_MODEL, SEQ, CHUNK = 2048, 256, 64
HEADS, HD = 8, 128
D_FF = 4 * D_MODEL
EPS, GN_EPS = 1e-6, 1e-5
ROPE_BASE = 10000.0
MT = SEQ // P
KT = D_MODEL // P
N_ATT, N_RET, N = 3 * HD, 4 * HD, 512
SLAB_KT = 4
SLABS = KT // SLAB_KT
PIECES = 8
PIECE_KT = KT // PIECES
SLOTS = 4
AHEAD = 2
OUT_GROUPS = D_MODEL // N
WARM_UP = 13
FF_ROUNDS = D_FF // D_MODEL
G_OUT = 2 * HEADS
G_FF = G_OUT + OUT_GROUPS
SCORE_COLS = SEQ + P
MIX_ORDER = list(range(HEADS, 2 * HEADS)) + list(range(HEADS))
GV_NORM1, GV_NORM2, GV_RET, GV_Q, GV_K = 0, KT, 2 * KT, 2 * KT + HEADS, 2 * KT + HEADS + 1
GV = GV_K + 1


def hybrid_block(nc, x, x_cols, w_att, w_ret, w_out, w_up, w_down, gains, rel_windows, rope_cos, rope_sin, decay, out):
    f32, f32r = mybir.dt.float32, mybir.dt.float32r
    ALU, ACT, AX = mybir.AluOpType, mybir.ActivationFunctionType, mybir.AxisListType

    with ExitStack() as ctx:
        def sb(name, shape, dt=f32):
            return ctx.enter_context(nc.sbuf_tensor(name, shape, dt))

        def sem(name):
            return ctx.enter_context(nc.semaphore(name))

        xs = sb("xs", [P, MT, D_MODEL])
        hT_hi = sb("hT_hi", [P, KT, SEQ], f32r)
        hT_lo = sb("hT_lo", [P, KT, SEQ], f32r)
        zT_hi = sb("zT_hi", [P, KT, SEQ], f32r)
        zT_lo = sb("zT_lo", [P, KT, SEQ], f32r)
        raw = sb("raw", [P, SLABS, SLAB_KT * N])
        w_hi = sb("w_hi", [P, SLOTS, PIECE_KT * N], f32r)
        w_lo = sb("w_lo", [P, SLOTS, PIECE_KT * N], f32r)
        gv = sb("gv", [P, GV])
        gq = sb("gq", [P, 1])
        cosb = sb("cosb", [P, MT, HD])
        sinb = sb("sinb", [P, MT, HD])
        dec = sb("dec", [P, HEADS, SCORE_COLS])
        bias = sb("bias", [P, HEADS, 2 * P])
        ident = sb("ident", [P, P])
        neg_half = sb("neg_half", [P, 4])
        junk = sb("junk", [P, N])
        ss = sb("ss", [P, MT, OUT_GROUPS])
        ms = sb("ms", [P, MT])
        me = sb("me", [P, MT])
        rstd1 = sb("rstd1", [P, MT])
        ss2 = sb("ss2", [P, MT, OUT_GROUPS])
        ms2 = sb("ms2", [P, MT])
        me2 = sb("me2", [P, MT])
        rstd2 = sb("rstd2", [P, MT])
        ap_ = sb("a_proj", [P, MT, N_ATT])
        a_ss = sb("a_ss", [P, 2 * MT])
        a_ms = sb("a_ms", [P, 2 * MT])
        a_rs = sb("a_rs", [P, 2 * MT])
        a_qk = sb("a_qk", [P, MT, 2 * HD])
        a_qT = sb("a_qT", [P, SEQ])
        a_kT = sb("a_kT", [P, SEQ])
        a_s = sb("a_s", [P, SCORE_COLS])
        a_mx = sb("a_mx", [P, MT])
        a_nmx = sb("a_nmx", [P, MT])
        a_e = sb("a_e", [P, SCORE_COLS])
        a_sum = sb("a_sum", [P, MT])
        a_rc = sb("a_rc", [P, MT])
        a_p = sb("a_p", [P, SCORE_COLS])
        a_pT = sb("a_pT", [P, SCORE_COLS])
        rp = sb("r_proj", [P, MT, N_RET])
        r_c = sb("r_c", [P, MT, 2 * HD])
        r_s = sb("r_s", [P, MT, 2 * HD])
        r_qk = sb("r_qk", [P, MT, 2 * HD])
        r_qT = sb("r_qT", [P, SEQ])
        r_kT = sb("r_kT", [P, SEQ])
        r_sT = sb("r_sT", [P, SCORE_COLS])
        r_st = sb("r_st", [P, MT, 6])
        r_mv = sb("r_mv", [P, MT, 2])
        r_ve = sb("r_ve", [P, MT])
        r_rs = sb("r_rs", [P, MT])
        r_eg = sb("r_eg", [P, MT, HD])
        r_eg1 = sb("r_eg1", [P, MT, HD])
        r_sg = sb("r_sg", [P, MT, HD])
        r_gate = sb("r_gate", [P, MT, HD])
        r_z = sb("r_z", [P, MT, HD])
        r_zn = sb("r_zn", [P, MT, HD])
        u = rp
        hid = sb("hid", [P, MT, N])
        xc = [hid[:].rearrange("p m n -> p (m n)")]
        xc += [dec[:].rearrange("p h n -> p (h n)")[:, b * SLAB_KT * SEQ:(b + 1) * SLAB_KT * SEQ] for b in range(3)]

        acc = [[ctx.enter_context(nc.psum_tensor(f"acc{p}{m}", [P, N], f32)) for m in range(MT)] for p in range(2)]
        bankA, bankB, bankC, bankD = [ctx.enter_context(nc.psum_tensor(f"bank{b}", [P, N], f32)) for b in "ABCD"]

        x_in = [sem(f"x_in{c}") for c in range(OUT_GROUPS)]
        xc_in = [sem(f"xc_in{q}") for q in range(PIECES)]
        half_in = [sem(f"half_in{s}") for s in range(SLABS)]
        gains_in = sem("gains_in")
        rope_in = sem("rope_in")
        decay_in = sem("decay_in")
        xc_hi = sem("xc_hi")
        xc_lo = sem("xc_lo")
        bias_in = sem("bias_in")
        slab_in = [sem(f"slab_in{s}") for s in range(SLABS)]
        hi_done = sem("hi_done")
        lo_done = sem("lo_done")
        piece_used = sem("piece_used")
        m0_done = sem("m0_done")
        acc_read_act = sem("acc_read_act")
        acc_read_dve = sem("acc_read_dve")
        zeroed = sem("zeroed")
        ident_ok = sem("ident_ok")
        half_ok = sem("half_ok")
        gq_ok = sem("gq_ok")
        mask_ok = sem("mask_ok")
        squared = sem("squared")
        squared_dve = sem("squared_dve")
        ms_ok = sem("ms_ok")
        me_ok = sem("me_ok")
        rstd1_ok = sem("rstd1_ok")
        tr_done = sem("tr_done")
        tr_hi = sem("tr_hi")
        tr_lo = sem("tr_lo")
        ms2_ok = sem("ms2_ok")
        me2_ok = sem("me2_ok")
        rstd2_ok = sem("rstd2_ok")
        a_ss_ok = sem("a_ss_ok")
        a_ms_ok = sem("a_ms_ok")
        a_rs_ok = sem("a_rs_ok")
        a_qk_ok = sem("a_qk_ok")
        a_T = sem("a_T")
        a_qT_ok = sem("a_qT_ok")
        a_kT_ok = sem("a_kT_ok")
        a_scores = sem("a_scores")
        a_s_ok = sem("a_s_ok")
        a_mx_ok = sem("a_mx_ok")
        a_nmx_ok = sem("a_nmx_ok")
        a_exp_ok = sem("a_exp_ok")
        a_rc_ok = sem("a_rc_ok")
        a_p_ok = sem("a_p_ok")
        a_PT = sem("a_PT")
        a_pT_ok = sem("a_pT_ok")
        a_pv = sem("a_pv")
        a_mix_hi = sem("a_mix_hi")
        a_mix_lo = sem("a_mix_lo")
        r_cs_ok = sem("r_cs_ok")
        r_qk_ok = sem("r_qk_ok")
        r_T = sem("r_T")
        r_qT_ok = sem("r_qT_ok")
        r_kT_ok = sem("r_kT_ok")
        r_scores = sem("r_scores")
        r_sT_ok = sem("r_sT_ok")
        r_y = sem("r_y")
        r_st_ok = sem("r_st_ok")
        r_mv_ok = sem("r_mv_ok")
        r_ve_ok = sem("r_ve_ok")
        r_rs_ok = sem("r_rs_ok")
        r_eg_ok = sem("r_eg_ok")
        r_eg1_ok = sem("r_eg1_ok")
        r_sg_ok = sem("r_sg_ok")
        r_gate_ok = sem("r_gate_ok")
        r_z_ok = sem("r_z_ok")
        r_zn_ok = sem("r_zn_ok")
        r_ZT = sem("r_ZT")
        r_mix_hi = sem("r_mix_hi")
        r_mix_lo = sem("r_mix_lo")
        hid_ok = sem("hid_ok")
        stored = sem("stored")

        def piece_cols(n):
            return PIECE_KT * n

        def tile_cols(m):
            return slice(m * P, (m + 1) * P)

        EngineType = mybir.EngineType

        def loop(engine, start, end):
            return nc.Fori(start, end, engines=(engine,), hint_back_edge=True)

        block = ctx.enter_context(nc.Block())

        @block.sync
        def _(sp):
            def load_slab(g, s, src, n):
                if not isinstance(g, int) or g > 0:
                    sp.wait_ge(lo_done, 8 * g - 8 + 2 * s + 2)
                sp.dma_start(raw[:, s, 0:SLAB_KT * n], src).then_inc(slab_in[s], 16)

            def load_group(g, table, index, n):
                for s in range(SLABS):
                    load_slab(g, s, table[bass.ds(index * (SLABS * P) + s * P, P), :], n)

            half_x, half_w = PIECE_KT * SEQ, PIECE_KT * N_ATT
            x_pieces = x_cols.rearrange("p k t -> p (k t)")
            for q in range(PIECES):
                s, o = q // 2, q % 2
                sp.dma_start(xc[s][:, o * half_x:(o + 1) * half_x],
                             x_pieces[:, q * half_x:(q + 1) * half_x]).then_inc(xc_in[q], 16)
                sp.dma_start(raw[:, s, o * half_w:(o + 1) * half_w],
                             w_att[s * P:(s + 1) * P, o * half_w:(o + 1) * half_w]).then_inc(
                                 slab_in[s] if o else half_in[s], 16)
                if q == 0:
                    sp.dma_start(gv[:], gains).then_inc(gains_in, 16)
            x_rows = x.rearrange("b (m p) d -> p (b m) d", p=P)
            for c in range(OUT_GROUPS):
                sp.dma_start(xs[:, :, c * N:(c + 1) * N], x_rows[:, :, c * N:(c + 1) * N]).then_inc(x_in[c], 16)
                if c == 0:
                    load_slab(1, 0, w_ret[0:P, :], N_RET)
            load_slab(1, 1, w_ret[P:2 * P, :], N_RET)
            load_slab(1, 2, w_ret[2 * P:3 * P, :], N_RET)
            sp.dma_start(bias[:], rel_windows).then_inc(bias_in, 16)
            load_slab(1, 3, w_ret[3 * P:4 * P, :], N_RET)
            sp.dma_start(cosb[:], rope_cos.rearrange("(m p) d -> p m d", p=P)).then_inc(rope_in, 16)
            sp.dma_start(sinb[:], rope_sin.rearrange("(m p) d -> p m d", p=P)).then_inc(rope_in, 16)
            sp.wait_ge(xc_lo, KT // 2)
            sp.dma_start(dec[:], decay).then_inc(decay_in, 16)
            with sp.Fori(1, HEADS) as h:
                load_group(2 * h, w_att, h, N_ATT)
                load_group(2 * h + 1, w_ret, h, N_RET)
            with sp.Fori(0, OUT_GROUPS) as c:
                load_group(G_OUT + c, w_out, c, N)
            with sp.Fori(0, FF_ROUNDS) as g:
                for c in range(4):
                    load_group(G_FF + 8 * g + c, w_up, 4 * g + c, N)
                for c in range(4):
                    load_group(G_FF + 8 * g + 4 + c, w_down, 4 * g + c, N)
            out_rows = out.rearrange("b (m p) d -> p (b m) d", p=P)
            for c in range(4):
                for m in range(MT):
                    sp.wait_ge(acc_read_dve, 2 * (OUT_GROUPS + 4 * (FF_ROUNDS - 1) + c) + m + 1)
                    sp.dma_start(out_rows[:, m, c * N:(c + 1) * N], xs[:, m, c * N:(c + 1) * N]).then_inc(stored, 16)
            sp.wait_ge(stored, 4 * MT * 16)

        @block.gpsimd
        def _(pool):
            nc.gpsimd.memset(neg_half[:], -0.5).then_inc(half_ok, 1)
            nc.gpsimd.memset(ident[:], 0.0).then_inc(zeroed, 1)
            pool.wait_ge(zeroed, 1)
            nc.gpsimd.affine_select(out=ident[:], in_=ident[:], compare_op=ALU.not_equal, fill=1.0, base=0,
                                    pattern=[[-1, P]], channel_multiplier=1).then_inc(ident_ok, 1)
            pool.wait_ge(half_ok, 1)
            pool.wait_ge(me_ok, 1)
            nc.gpsimd.tensor_tensor(rstd1[:], me[:], neg_half[:, 0:MT], ALU.pow).then_inc(rstd1_ok, 1)
            pool.wait_ge(bias_in, 16)
            nc.gpsimd.memset(bias[0:CHUNK, :, P + CHUNK:2 * P], -1e30).then_inc(mask_ok, 1)

            def att_power(h):
                pool.wait_ge(a_ms_ok, h + 1)
                nc.gpsimd.tensor_tensor(a_rs[:], a_ms[:], neg_half[:], ALU.pow).then_inc(a_rs_ok, 1)

            def ret_power(h):
                pool.wait_ge(r_ve_ok, h + 1)
                nc.gpsimd.tensor_tensor(r_rs[:], r_ve[:], neg_half[:, 0:MT], ALU.pow).then_inc(r_rs_ok, 1)

            with pool.Fori(0, HEADS) as h:
                att_power(h)
                ret_power(h)
            pool.wait_ge(me2_ok, 1)
            nc.gpsimd.tensor_tensor(rstd2[:], me2[:], neg_half[:, 0:MT], ALU.pow).then_inc(rstd2_ok, 1)

        PAIRS = KT // 2

        @block.tensor
        def _(pe):
            def group(g, par, hi, lo, order, n, acc_free, work):
                for j in range(PIECES):
                    pe.wait_ge(lo_done, 8 * g + j + 1)
                    for m in range(MT):
                        if j == 0:
                            acc_free(m)
                        for t in range(PIECE_KT):
                            k = order[PIECE_KT * j + t]
                            first, last = (j == 0 and t == 0), (j == PIECES - 1 and t == PIECE_KT - 1)
                            wh = w_hi[:, j % SLOTS, t * n:(t + 1) * n]
                            wl = w_lo[:, j % SLOTS, t * n:(t + 1) * n]
                            o = acc[par][m][:, 0:n]
                            nc.tensor.matmul(o, hi[:, k, tile_cols(m)], wh, start=first, stop=False)
                            nc.tensor.matmul(o, hi[:, k, tile_cols(m)], wl, start=False, stop=False)
                            mm = nc.tensor.matmul(o, lo[:, k, tile_cols(m)], wh, start=False, stop=last)
                        if j == PIECES - 1 and m == 0:
                            mm.then_inc(m0_done, 1)
                    mm.then_inc(piece_used, 1)
                    for f in work.get(j, ()):
                        f()

            def free_by_act(groups):
                return lambda m: pe.wait_ge(acc_read_act, 2 * groups + m + 1)

            def free_by_dve(groups):
                return lambda m: pe.wait_ge(acc_read_dve, 2 * groups + m + 1)

            def unused(m):
                pass

            def transpose_pair(e, src, ready):
                ready()
                if not isinstance(e, int) or e >= 2:
                    pe.wait_ge(tr_lo, e - 1)
                bank = bankB if EVEN[0] else bankA
                EVEN[0] = not EVEN[0]
                for t in range(2):
                    for m in range(MT):
                        mm = nc.tensor.transpose(bank[:, (2 * t + m) * P:(2 * t + m + 1) * P],
                                                 src(m)[:, t * P:(t + 1) * P], ident[:])
                mm.then_inc(tr_done, 1)

            def att_T(h):
                pe.wait_ge(a_qk_ok, h + 1)
                for m in range(MT):
                    nc.tensor.transpose(bankA[:, tile_cols(m)], a_qk[:, m, 0:HD], ident[:])
                for m in range(MT):
                    mm = nc.tensor.transpose(bankB[:, tile_cols(m)], a_qk[:, m, HD:2 * HD], ident[:])
                mm.then_inc(a_T, 1)

            def att_scores(h):
                pe.wait_ge(a_qT_ok, h + 1)
                pe.wait_ge(a_kT_ok, h + 1)
                nc.tensor.matmul(bankC[:, 0:P], a_qT[:, 0:P], a_kT[:, 0:P], start=True, stop=True)
                nc.tensor.matmul(bankC[:, P:P + SEQ], a_qT[:, P:SEQ], a_kT[:, 0:SEQ],
                                 start=True, stop=True).then_inc(a_scores, 1)

            def att_PT(h):
                pe.wait_ge(a_p_ok, h + 1)
                for b in range(3):
                    mm = nc.tensor.transpose(bankD[:, b * P:(b + 1) * P], a_p[:, b * P:(b + 1) * P], ident[:])
                mm.then_inc(a_PT, 1)

            def att_pv(h):
                pe.wait_ge(a_pT_ok, h + 1)
                nc.tensor.matmul(bankC[:, 0:SEQ], ap_[:, 0, 2 * HD:3 * HD], a_pT[:, 0:SEQ], start=True, stop=False)
                nc.tensor.matmul(bankC[:, P:SEQ], ap_[:, 1, 2 * HD:3 * HD], a_pT[:, SEQ:SEQ + P],
                                 start=False, stop=True).then_inc(a_pv, 1)

            def ret_T(h):
                pe.wait_ge(r_qk_ok, h + 1)
                for m in range(MT):
                    nc.tensor.transpose(bankA[:, tile_cols(m)], r_qk[:, m, 0:HD], ident[:])
                for m in range(MT):
                    mm = nc.tensor.transpose(bankB[:, tile_cols(m)], r_qk[:, m, HD:2 * HD], ident[:])
                mm.then_inc(r_T, 1)

            def ret_scores(h):
                pe.wait_ge(r_qT_ok, h + 1)
                pe.wait_ge(r_kT_ok, h + 1)
                nc.tensor.matmul(bankD[:, 0:SEQ], r_kT[:, 0:P], r_qT[:, 0:SEQ], start=True, stop=True)
                nc.tensor.matmul(bankD[:, SEQ:SEQ + P], r_kT[:, P:SEQ], r_qT[:, P:SEQ],
                                 start=True, stop=True).then_inc(r_scores, 1)

            def ret_y(h):
                pe.wait_ge(r_sT_ok, h + 1)
                v = [rp[:, m, 2 * HD:3 * HD] for m in range(MT)]
                nc.tensor.matmul(bankC[:, 0:P], r_sT[:, 0:P], v[0], start=True, stop=True)
                nc.tensor.matmul(bankC[:, P:SEQ], r_sT[:, P:SEQ], v[0], start=True, stop=False)
                nc.tensor.matmul(bankC[:, P:SEQ], r_sT[:, SEQ:SEQ + P], v[1], start=False, stop=True).then_inc(r_y, 1)

            def ret_ZT(h):
                pe.wait_ge(r_zn_ok, h + 1)
                for m in range(MT):
                    mm = nc.tensor.transpose(bankA[:, tile_cols(m)], r_zn[:, m, :], ident[:])
                mm.then_inc(r_ZT, 1)

            def att_work(h):
                return {4: [lambda: att_T(h)], 5: [lambda: att_scores(h)], 7: [lambda: att_PT(h)]}

            def ret_work(h):
                return {0: [lambda: att_pv(h)], 3: [lambda: ret_T(h)], 4: [lambda: ret_scores(h)],
                        5: [lambda: ret_y(h)], 7: [lambda: ret_ZT(h)]}

            in_order = list(range(KT))
            EVEN = [False]
            pe.wait_ge(ident_ok, 1)
            for _ in range(WARM_UP):
                nc.tensor.matmul(bankD[:, 0:P], ident[:], ident[:], start=True, stop=True)

            group(0, 0, hT_hi, hT_lo, in_order, N_ATT, unused, {})
            group(1, 1, hT_hi, hT_lo, in_order, N_RET, unused, att_work(0))
            group(2, 0, hT_hi, hT_lo, in_order, N_ATT, free_by_act(0), ret_work(0))
            with loop(EngineType.PE, 1, HEADS - 1) as i:
                group(2 * i + 1, 1, hT_hi, hT_lo, in_order, N_RET, free_by_act(2 * i - 1), att_work(i))
                group(2 * i + 2, 0, hT_hi, hT_lo, in_order, N_ATT, free_by_act(2 * i), ret_work(i))
            group(G_OUT - 1, 1, hT_hi, hT_lo, in_order, N_RET, free_by_act(G_OUT - 3), att_work(HEADS - 1))

            work = ret_work(HEADS - 1)
            work = {0: work[0], 1: work[3], 2: work[4], 3: work[5],
                    5: work[7] + [lambda: pe.wait_ge(r_mix_lo, HEADS - 1)],
                    6: [lambda: pe.wait_ge(r_mix_lo, HEADS)]}
            work[1] = work[1] + [lambda: pe.wait_ge(a_mix_lo, HEADS)]

            def stream_pairs(c):
                for b in range(2):
                    transpose_pair(2 * c + b,
                                   lambda m: xs[:, m, c * N + 2 * b * P:c * N + 2 * (b + 1) * P],
                                   lambda: pe.wait_ge(acc_read_dve, 2 * (c + 1)))

            for c in range(OUT_GROUPS):
                free = [free_by_act(G_OUT - 2), free_by_act(G_OUT - 1), free_by_dve(0), free_by_dve(1)][c]
                group(G_OUT + c, c % 2, zT_hi, zT_lo, MIX_ORDER, N, free,
                      work if c == 0 else {1: [lambda: stream_pairs(c - 1)]})

            def hidden_pairs(g, c):
                for b in range(2):
                    transpose_pair(PAIRS + 8 * g + 2 * c + b,
                                   lambda m: hid[:, m, 2 * b * P:2 * (b + 1) * P],
                                   lambda: pe.wait_ge(hid_ok, 2 * (4 * g + c) + 2))

            with loop(EngineType.PE, 0, FF_ROUNDS) as g:
                up, down = G_FF + 8 * g, G_FF + 8 * g + 4
                acts, dves = G_OUT + 4 * g, OUT_GROUPS + 4 * g

                def last_stream_pairs():
                    with pe.If(g < 1):
                        stream_pairs(OUT_GROUPS - 1)

                group(up, 0, hT_hi, hT_lo, in_order, N, free_by_dve(dves - 2),
                      {1: [last_stream_pairs],
                       5: [lambda: pe.wait_ge(tr_lo, PAIRS)]})
                group(up + 1, 1, hT_hi, hT_lo, in_order, N, free_by_dve(dves - 1), {2: [lambda: hidden_pairs(g, 0)]})
                group(up + 2, 0, hT_hi, hT_lo, in_order, N, free_by_act(acts), {2: [lambda: hidden_pairs(g, 1)]})
                group(up + 3, 1, hT_hi, hT_lo, in_order, N, free_by_act(acts + 1), {2: [lambda: hidden_pairs(g, 2)]})
                group(down, 0, zT_hi, zT_lo, in_order, N, free_by_act(acts + 2),
                      {2: [lambda: hidden_pairs(g, 3)],
                       5: [lambda: pe.wait_ge(tr_lo, PAIRS + 8 * g + 8)]})
                group(down + 1, 1, zT_hi, zT_lo, in_order, N, free_by_act(acts + 3), {})
                group(down + 2, 0, zT_hi, zT_lo, in_order, N, free_by_dve(dves), {})
                group(down + 3, 1, zT_hi, zT_lo, in_order, N, free_by_dve(dves + 1), {})

        @block.scalar
        def _(act):
            def hi_piece(g, q, n):
                if isinstance(g, int) and g == 0:
                    act.wait_ge(slab_in[q // 2] if q % 2 else half_in[q // 2], 16)
                elif q % 2 == 0:
                    act.wait_ge(slab_in[q // 2], 16 * g + 16)
                if not isinstance(g, int) or 8 * g + q >= SLOTS:
                    act.wait_ge(piece_used, 8 * g + q + 1 - SLOTS)
                nc.scalar.activation(w_hi[:, q % SLOTS, 0:PIECE_KT * n],
                                     raw[:, q // 2, (q % 2) * PIECE_KT * n:(q % 2 + 1) * PIECE_KT * n],
                                     ACT.Copy).then_inc(hi_done, 1)

            def group(g, n, n_next, work):
                for j in range(PIECES):
                    if j + AHEAD < PIECES:
                        hi_piece(g, j + AHEAD, n)
                    elif n_next:
                        hi_piece(g + 1, j + AHEAD - PIECES, n_next)
                    for f in work.get(j, ()):
                        f()

            def evacuate(g, par, m, dst, func, scale):
                if m == 0:
                    act.wait_ge(m0_done, g + 1)
                else:
                    act.wait_ge(piece_used, 8 * g + 8)
                n = dst.shape[-1]
                nc.scalar.activation(dst, acc[par][m][:, 0:n], func, scale=scale).then_inc(acc_read_act, 1)

            def att_proj(h):
                act.wait_ge(rstd1_ok, 1)
                for m in range(MT):
                    evacuate(2 * h, 0, m, ap_[:, m, :], ACT.Copy, rstd1[:, m:m + 1])

            def att_squares(h):
                act.wait_ge(acc_read_act, 4 * h + 2)
                for m in range(MT):
                    for s in range(2):
                        i = 2 * m + s
                        ins = nc.scalar.activation(junk[:, i * HD:(i + 1) * HD], ap_[:, m, s * HD:(s + 1) * HD],
                                                   ACT.Square, scale=HD ** -0.5, accum_out=a_ss[:, i:i + 1])
                ins.then_inc(a_ss_ok, 1)

            def att_qT(h):
                act.wait_ge(a_T, h + 1)
                nc.scalar.activation(a_qT[:], bankA[:, 0:SEQ], ACT.Copy, scale=gq[:, 0:1]).then_inc(a_qT_ok, 1)

            def att_exp(h):
                act.wait_ge(a_nmx_ok, h + 1)
                nc.scalar.activation(a_e[:, 0:P], a_s[:, 0:P], ACT.Exp, bias=a_nmx[:, 0:1], accum_out=a_sum[:, 0:1])
                nc.scalar.activation(a_e[:, P:P + SEQ], a_s[:, P:P + SEQ], ACT.Exp, bias=a_nmx[:, 1:2],
                                     accum_out=a_sum[:, 1:2]).then_inc(a_exp_ok, 1)

            def att_pT(h):
                act.wait_ge(a_PT, h + 1)
                nc.scalar.activation(a_pT[:], bankD[:, 0:SCORE_COLS], ACT.Copy).then_inc(a_pT_ok, 1)

            def att_mix(h):
                act.wait_ge(a_pv, h + 1)
                nc.scalar.activation(zT_hi[:, HEADS + h, :], bankC[:, 0:SEQ], ACT.Copy).then_inc(a_mix_hi, 1)

            def ret_proj(h):
                for m in range(MT):
                    evacuate(2 * h + 1, 1, m, rp[:, m, :], ACT.Copy, rstd1[:, m:m + 1])

            def ret_exp(h):
                act.wait_ge(acc_read_act, 4 * h + 4)
                nc.scalar.activation(r_eg[:], rp[:, :, 3 * HD:4 * HD], ACT.Exp, scale=-1.0).then_inc(r_eg_ok, 1)

            def ret_qT(h):
                act.wait_ge(r_T, h + 1)
                nc.scalar.activation(r_qT[:], bankA[:, 0:SEQ], ACT.Copy).then_inc(r_qT_ok, 1)

            def ret_scale(h):
                act.wait_ge(r_z_ok, h + 1)
                act.wait_ge(r_rs_ok, h + 1)
                for m in range(MT):
                    ins = nc.scalar.activation(r_zn[:, m, :], r_z[:, m, :], ACT.Copy, scale=r_rs[:, m:m + 1])
                ins.then_inc(r_zn_ok, 1)

            def ret_mix(h):
                act.wait_ge(r_ZT, h + 1)
                nc.scalar.activation(zT_hi[:, h, :], bankA[:, 0:SEQ], ACT.Copy,
                                     scale=gv[:, bass.ds(h + GV_RET, 1)]).then_inc(r_mix_hi, 1)

            def att_work(h):
                return {0: [lambda: att_proj(h)], 1: [lambda: att_squares(h)], 4: [lambda: att_qT(h)],
                        6: [lambda: att_exp(h)], 7: [lambda: att_pT(h)]}

            def ret_work(h):
                return {0: [lambda: ret_proj(h), lambda: att_mix(h)], 2: [lambda: ret_exp(h)],
                        3: [lambda: ret_qT(h)], 6: [lambda: ret_scale(h)], 7: [lambda: ret_mix(h)]}

            def pair_hi(e, dst_k, gain):
                act.wait_ge(tr_done, e + 1)
                bank = bankB if EVEN[0] else bankA
                EVEN[0] = not EVEN[0]
                dst = zT_hi if gain is None else hT_hi
                if gain is None:
                    nc.scalar.activation(dst[:, dst_k:dst_k + 2, :].rearrange("p k t -> p (k t)"), bank[:],
                                         ACT.Copy).then_inc(tr_hi, 1)
                    return
                for t in range(2):
                    ins = nc.scalar.activation(dst[:, dst_k + t, :], bank[:, t * SEQ:(t + 1) * SEQ], ACT.Copy,
                                               scale=gv[:, gain + dst_k + t:gain + dst_k + t + 1])
                ins.then_inc(tr_hi, 1)

            def x_hi(e):
                act.wait_ge(xc_in[e], 16)
                for k in range(2 * e, 2 * e + 2):
                    ins = nc.scalar.activation(hT_hi[:, k, :], xc[e // 2][:, (k % SLAB_KT) * SEQ:(k % SLAB_KT + 1) * SEQ],
                                               ACT.Copy, scale=gv[:, GV_NORM1 + k:GV_NORM1 + k + 1])
                ins.then_inc(xc_hi, 1)

            EVEN = [False]
            act.wait_ge(half_ok, 1)
            nc.scalar.activation(a_nmx[:], neg_half[:, 0:MT], ACT.Exp)
            act.wait_ge(gains_in, 16)
            for e in range(AHEAD):
                x_hi(e)
                hi_piece(0, e, N_ATT)
            work = {j: [lambda e=j + AHEAD: x_hi(e)] for j in range(PIECES - AHEAD)}

            def squares(m, c, sums, before):
                if before:
                    act.wait_ge(squared, before)
                nc.scalar.activation(junk[:], xs[:, m, c * N:(c + 1) * N], ACT.Square, scale=D_MODEL ** -0.5,
                                     accum_out=sums[:, m, c:c + 1]).then_inc(squared, 1)

            def x_squares():
                for c in range(OUT_GROUPS):
                    act.wait_ge(x_in[c], 16)
                    squares(0, c, ss, c)

            work[PIECES - 1] = [x_squares]
            group(0, N_ATT, N_RET, work)
            act.wait_ge(gq_ok, 1)
            with loop(EngineType.Activation, 0, HEADS - 1) as i:
                group(2 * i + 1, N_RET, N_ATT, att_work(i))
                group(2 * i + 2, N_ATT, N_RET, ret_work(i))
            group(G_OUT - 1, N_RET, N, att_work(HEADS - 1))

            work = ret_work(HEADS - 1)
            work = {0: work[0] + work[2], 1: work[3], 4: work[6], 5: work[7]}
            group(G_OUT, N, N, work)

            def stream_split(c):
                for b in range(2):
                    pair_hi(2 * c + b, 4 * c + 2 * b, GV_NORM2)
                act.wait_ge(acc_read_dve, 2 * c + 2)
                for m in range(MT):
                    squares(m, c, ss2, OUT_GROUPS + MT * c + m)

            for c in range(1, OUT_GROUPS):
                group(G_OUT + c, N, N, {2: [lambda: stream_split(c - 1)]})

            def hidden_relu(g, c):
                act.wait_ge(rstd2_ok, 1)
                for m in range(MT):
                    evacuate(G_FF + 8 * g + c, c % 2, m, u[:, m, :], ACT.Relu, rstd2[:, m:m + 1])

            def hidden_split(g, c):
                for b in range(2):
                    pair_hi(PAIRS + 8 * g + 2 * c + b, 4 * c + 2 * b, None)

            with loop(EngineType.Activation, 0, FF_ROUNDS) as g:
                def first_pieces(q):
                    with act.If(g < FF_ROUNDS - 1):
                        hi_piece(G_FF + 8 * g + 8, q, N)

                def last_stream_split():
                    with act.If(g < 1):
                        stream_split(OUT_GROUPS - 1)

                for c in range(8):
                    work = {}
                    if c == 0:
                        work = {2: [last_stream_split]}
                    if c == 7:
                        work = {PIECES - AHEAD + q: [lambda q=q: first_pieces(q)] for q in range(AHEAD)}
                    if 1 <= c <= 4:
                        work = {0: [lambda: hidden_relu(g, c - 1)], 2: [lambda: hidden_split(g, c - 1)]}
                    group(G_FF + 8 * g + c, N, N if c < 7 else None, work)

        @block.vector
        def _(dve):
            def lo_piece(g, q, n):
                dve.wait_ge(hi_done, 8 * g + q + 1)
                nc.vector.tensor_tensor(w_lo[:, q % SLOTS, 0:PIECE_KT * n],
                                        raw[:, q // 2, (q % 2) * PIECE_KT * n:(q % 2 + 1) * PIECE_KT * n],
                                        w_hi[:, q % SLOTS, 0:PIECE_KT * n].bitcast(f32),
                                        ALU.subtract).then_inc(lo_done, 1)

            def group(g, n, n_next, work):
                for j in range(PIECES):
                    if j + AHEAD < PIECES:
                        lo_piece(g, j + AHEAD, n)
                    elif n_next:
                        lo_piece(g + 1, j + AHEAD - PIECES, n_next)
                    for f in work.get(j, ()):
                        f()

            def att_mean_squares(h):
                dve.wait_ge(a_ss_ok, h + 1)
                nc.vector.tensor_scalar(a_ms[:], a_ss[:], EPS, None, ALU.add).then_inc(a_ms_ok, 1)

            def att_norm(h):
                dve.wait_ge(a_rs_ok, h + 1)
                for m in range(MT):
                    for s in range(2):
                        i = 2 * m + s
                        ins = nc.vector.tensor_scalar(a_qk[:, m, s * HD:(s + 1) * HD], ap_[:, m, s * HD:(s + 1) * HD],
                                                      a_rs[:, i:i + 1], None, ALU.mult)
                ins.then_inc(a_qk_ok, 1)

            def att_kT(h):
                dve.wait_ge(a_T, h + 1)
                nc.vector.tensor_scalar(a_kT[:], bankB[:, 0:SEQ], gv[:, GV_K:GV_K + 1], None,
                                        ALU.mult).then_inc(a_kT_ok, 1)

            def att_bias_max(h):
                dve.wait_ge(mask_ok, 1)
                dve.wait_ge(a_scores, h + 1)
                hb = bias[:, bass.ds(h, 1), :].rearrange("p a k -> p (a k)")
                nc.vector.tensor_tensor(a_s[:, 0:P], bankC[:, 0:P], hb[:, P:2 * P], ALU.add)
                nc.vector.tensor_tensor(a_s[:, P:P + SEQ], bankC[:, P:P + SEQ], hb, ALU.add).then_inc(a_s_ok, 1)
                dve.wait_ge(a_s_ok, h + 1)
                nc.vector.tensor_reduce(a_mx[:, 0:1], a_s[:, 0:P], AX.X, ALU.max)
                nc.vector.tensor_reduce(a_mx[:, 1:2], a_s[:, P:P + SEQ], AX.X, ALU.max).then_inc(a_mx_ok, 1)
                dve.wait_ge(a_mx_ok, h + 1)
                nc.vector.tensor_scalar(a_nmx[:], a_mx[:], -1.0, None, ALU.mult).then_inc(a_nmx_ok, 1)

            def att_probs(h):
                dve.wait_ge(a_exp_ok, h + 1)
                nc.vector.reciprocal(a_rc[:], a_sum[:]).then_inc(a_rc_ok, 1)
                dve.wait_ge(a_rc_ok, h + 1)
                nc.vector.tensor_scalar(a_p[:, 0:P], a_e[:, 0:P], a_rc[:, 0:1], None, ALU.mult)
                nc.vector.tensor_scalar(a_p[:, P:P + SEQ], a_e[:, P:P + SEQ], a_rc[:, 1:2], None,
                                        ALU.mult).then_inc(a_p_ok, 1)

            def att_mix(h):
                dve.wait_ge(a_mix_hi, h + 1)
                nc.vector.tensor_tensor(zT_lo[:, HEADS + h, :], bankC[:, 0:SEQ],
                                        zT_hi[:, HEADS + h, :].bitcast(f32), ALU.subtract).then_inc(a_mix_lo, 1)

            def ret_rotate(h):
                dve.wait_ge(rope_in, 2 * 16)
                dve.wait_ge(acc_read_act, 4 * h + 4)
                for m in range(MT):
                    qk = rp[:, m, 0:2 * HD]
                    cos = cosb[:, m, :].rearrange("p (a d) -> p a d", a=1).to_broadcast([P, 2, HD])
                    nc.vector.tensor_tensor(r_c[:, m, :].rearrange("p (s d) -> p s d", s=2),
                                            qk.rearrange("p (s d) -> p s d", s=2), cos, ALU.mult)
                    for half in range(2):
                        src = qk.rearrange("p (s f d) -> p s f d", s=2, f=2)[:, :, 1 - half, :]
                        dst = r_s[:, m, :].rearrange("p (s f d) -> p s f d", s=2, f=2)[:, :, half, :]
                        sin = sinb[:, m, half * HD // 2:(half + 1) * HD // 2].rearrange("p (a d) -> p a d", a=1)
                        ins = nc.vector.tensor_tensor(dst, src, sin.to_broadcast([P, 2, HD // 2]), ALU.mult)
                ins.then_inc(r_cs_ok, 1)

            def ret_rotated(h):
                dve.wait_ge(r_cs_ok, h + 1)
                nc.vector.tensor_tensor(r_qk[:], r_c[:], r_s[:], ALU.add).then_inc(r_qk_ok, 1)

            def ret_kT(h):
                dve.wait_ge(r_T, h + 1)
                nc.vector.tensor_copy(r_kT[:], bankB[:, 0:SEQ]).then_inc(r_kT_ok, 1)

            def ret_sigmoid(h):
                dve.wait_ge(r_eg_ok, h + 1)
                nc.vector.tensor_scalar(r_eg1[:], r_eg[:], 1.0, None, ALU.add).then_inc(r_eg1_ok, 1)
                dve.wait_ge(r_eg1_ok, h + 1)
                nc.vector.reciprocal(r_sg[:], r_eg1[:]).then_inc(r_sg_ok, 1)

            def ret_decay(h):
                dve.wait_ge(decay_in, 16)
                dve.wait_ge(r_scores, h + 1)
                nc.vector.tensor_tensor(r_sT[:], bankD[:, 0:SCORE_COLS],
                                        dec[:, bass.ds(h, 1), :].rearrange("p a k -> p (a k)"),
                                        ALU.mult).then_inc(r_sT_ok, 1)

            def ret_norm(h):
                dve.wait_ge(r_y, h + 1)
                for m in range(MT):
                    ins = nc.vector.bn_stats(r_st[:, m, :], bankC[:, tile_cols(m)])
                ins.then_inc(r_st_ok, 1)
                dve.wait_ge(r_sg_ok, h + 1)
                dve.wait_ge(r_st_ok, h + 1)
                nc.vector.tensor_tensor(r_gate[:], rp[:, :, 3 * HD:4 * HD], r_sg[:], ALU.mult).then_inc(r_gate_ok, 1)
                for m in range(MT):
                    ins = nc.vector.bn_aggr(r_mv[:, m, :], r_st[:, m, :])
                ins.then_inc(r_mv_ok, 1)
                dve.wait_ge(r_mv_ok, h + 1)
                nc.vector.tensor_scalar(r_ve[:], r_mv[:, :, 1], GN_EPS, None, ALU.add).then_inc(r_ve_ok, 1)
                dve.wait_ge(r_gate_ok, h + 1)
                for m in range(MT):
                    ins = nc.vector.scalar_tensor_tensor(out=r_z[:, m, :], in0=bankC[:, tile_cols(m)],
                                                         scalar=r_mv[:, m, 0:1], in1=r_gate[:, m, :],
                                                         op0=ALU.subtract, op1=ALU.mult)
                ins.then_inc(r_z_ok, 1)

            def ret_mix(h):
                dve.wait_ge(r_mix_hi, h + 1)
                nc.vector.scalar_tensor_tensor(out=zT_lo[:, h, :], in0=bankA[:, 0:SEQ],
                                               scalar=gv[:, bass.ds(h + GV_RET, 1)],
                                               in1=zT_hi[:, h, :].bitcast(f32),
                                               op0=ALU.mult, op1=ALU.subtract).then_inc(r_mix_lo, 1)

            def att_work(h):
                return {2: [lambda: att_mean_squares(h)], 3: [lambda: att_norm(h)], 4: [lambda: att_kT(h)],
                        5: [lambda: att_bias_max(h)], 6: [lambda: att_probs(h)]}

            def ret_work(h):
                return {0: [lambda: att_mix(h)], 1: [lambda: ret_rotate(h)], 2: [lambda: ret_rotated(h)],
                        3: [lambda: ret_kT(h), lambda: ret_sigmoid(h)], 4: [lambda: ret_decay(h)],
                        5: [lambda: ret_norm(h)], 7: [lambda: ret_mix(h)]}

            def pair_lo(e, dst_k, gain):
                dve.wait_ge(tr_hi, e + 1)
                bank = bankB if EVEN[0] else bankA
                EVEN[0] = not EVEN[0]
                if gain is None:
                    nc.vector.tensor_tensor(zT_lo[:, dst_k:dst_k + 2, :].rearrange("p k t -> p (k t)"), bank[:],
                                            zT_hi[:, dst_k:dst_k + 2, :].rearrange("p k t -> p (k t)").bitcast(f32),
                                            ALU.subtract).then_inc(tr_lo, 1)
                    return
                for t in range(2):
                    ins = nc.vector.scalar_tensor_tensor(out=hT_lo[:, dst_k + t, :], in0=bank[:, t * SEQ:(t + 1) * SEQ],
                                                         scalar=gv[:, gain + dst_k + t:gain + dst_k + t + 1],
                                                         in1=hT_hi[:, dst_k + t, :].bitcast(f32),
                                                         op0=ALU.mult, op1=ALU.subtract)
                ins.then_inc(tr_lo, 1)

            def x_lo(e):
                dve.wait_ge(xc_hi, e + 1)
                for k in range(2 * e, 2 * e + 2):
                    ins = nc.vector.scalar_tensor_tensor(
                        out=hT_lo[:, k, :], in0=xc[e // 2][:, (k % SLAB_KT) * SEQ:(k % SLAB_KT + 1) * SEQ],
                        scalar=gv[:, GV_NORM1 + k:GV_NORM1 + k + 1], in1=hT_hi[:, k, :].bitcast(f32),
                        op0=ALU.mult, op1=ALU.subtract)
                ins.then_inc(xc_lo, 1)

            EVEN = [False]
            dve.wait_ge(gains_in, 16)
            nc.vector.tensor_scalar(gq[:], gv[:, GV_Q:GV_Q + 1], HD ** -0.5, None, ALU.mult).then_inc(gq_ok, 1)
            for e in range(AHEAD):
                x_lo(e)
                lo_piece(0, e, N_ATT)

            def x_mean_squares():
                for c in range(OUT_GROUPS):
                    dve.wait_ge(x_in[c], 16)
                    cols = xs[:, 1, c * N:(c + 1) * N]
                    nc.vector.tensor_tensor_reduce(rp[:, c % MT, :], cols, cols, 1.0 / D_MODEL, 0.0,
                                                   ALU.mult, ALU.add, ss[:, 1, c:c + 1]).then_inc(squared_dve, 1)
                    if c:
                        dve.wait_ge(squared_dve, c)
                dve.wait_ge(squared_dve, OUT_GROUPS)
                dve.wait_ge(squared, OUT_GROUPS)
                nc.vector.tensor_reduce(ms[:], ss[:], AX.X, ALU.add).then_inc(ms_ok, 1)
                dve.wait_ge(ms_ok, 1)
                nc.vector.tensor_scalar(me[:], ms[:], EPS, None, ALU.add).then_inc(me_ok, 1)

            for j in range(PIECES):
                if j + AHEAD < PIECES:
                    x_lo(j + AHEAD)
                    lo_piece(0, j + AHEAD, N_ATT)
                else:
                    lo_piece(1, j + AHEAD - PIECES, N_RET)
            x_mean_squares()
            with loop(EngineType.DVE, 0, HEADS - 1) as i:
                group(2 * i + 1, N_RET, N_ATT, att_work(i))
                group(2 * i + 2, N_ATT, N_RET, ret_work(i))
            group(G_OUT - 1, N_RET, N, att_work(HEADS - 1))
            work = ret_work(HEADS - 1)
            work = {0: work[0] + work[1] + work[2], 1: work[3], 2: work[4], 3: work[5], 5: work[7]}
            group(G_OUT, N, N, work)

            def add_to_stream(g, par, c):
                for m in range(MT):
                    if m == 0:
                        dve.wait_ge(m0_done, g + 1)
                    else:
                        dve.wait_ge(piece_used, 8 * g + 8)
                    cols = xs[:, m, c * N:(c + 1) * N]
                    nc.vector.tensor_tensor(cols, acc[par][m][:], cols, ALU.add).then_inc(acc_read_dve, 1)

            def stream_split(c):
                for b in range(2):
                    pair_lo(2 * c + b, 4 * c + 2 * b, GV_NORM2)

            for c in range(1, OUT_GROUPS):
                group(G_OUT + c, N, N,
                      {0: [lambda: add_to_stream(G_OUT + c - 1, (c - 1) % 2, c - 1)], 2: [lambda: stream_split(c - 1)]})

            def stream_mean_squares():
                dve.wait_ge(squared, OUT_GROUPS + MT * OUT_GROUPS)
                nc.vector.tensor_reduce(ms2[:], ss2[:], AX.X, ALU.add).then_inc(ms2_ok, 1)
                dve.wait_ge(ms2_ok, 1)
                nc.vector.tensor_scalar(me2[:], ms2[:], EPS, None, ALU.add).then_inc(me2_ok, 1)

            def hidden_square(g, c):
                dve.wait_ge(acc_read_act, 2 * (G_OUT + 4 * g + c) + 2)
                for m in range(MT):
                    nc.vector.tensor_tensor(hid[:, m, :], u[:, m, :], u[:, m, :], ALU.mult).then_inc(hid_ok, 1)

            def hidden_split(g, c):
                for b in range(2):
                    pair_lo(PAIRS + 8 * g + 2 * c + b, 4 * c + 2 * b, None)

            with loop(EngineType.DVE, 0, FF_ROUNDS) as g:
                def first_pieces(q):
                    with dve.If(g < FF_ROUNDS - 1):
                        lo_piece(G_FF + 8 * g + 8, q, N)

                def last_stream_split():
                    with dve.If(g < 1):
                        stream_split(OUT_GROUPS - 1)

                def last_mean_squares():
                    with dve.If(g < 1):
                        stream_mean_squares()

                for c in range(8):
                    work = {}
                    if c == 0:
                        work = {0: [lambda: add_to_stream(G_FF + 8 * g - 1, 1, OUT_GROUPS - 1)],
                                2: [last_stream_split], 4: [last_mean_squares]}
                    if 1 <= c <= 4:
                        work = {1: [lambda: hidden_square(g, c - 1)], 2: [lambda: hidden_split(g, c - 1)]}
                    if c >= 5:
                        work = {0: [lambda: add_to_stream(G_FF + 8 * g + c - 1, (c - 1) % 2, c - 5)]}
                    if c == 7:
                        work |= {PIECES - AHEAD + q: [lambda q=q: first_pieces(q)] for q in range(AHEAD)}
                    group(G_FF + 8 * g + c, N, N if c < 7 else None, work)
            add_to_stream(G_FF + 8 * FF_ROUNDS - 1, 1, OUT_GROUPS - 1)


def tables():
    f32 = np.float32
    half = HD // 2
    inv_freq = (ROPE_BASE ** (-np.arange(half, dtype=f32) / half)).astype(f32)
    angle = (np.arange(SEQ, dtype=f32)[:, None] * inv_freq[None, :]).astype(f32)
    cos, sin = np.cos(angle).astype(f32), np.sin(angle).astype(f32)
    log_g = np.log1p(-np.exp2(-(5.0 + np.arange(HEADS))))
    key, query = np.arange(SEQ)[:, None], np.arange(SEQ)[None, :]
    full = np.exp(log_g[:, None, None] * np.abs(query - key)) * (key // CHUNK <= query // CHUNK) * HD ** -0.5
    decay = np.concatenate([full[:, 0:P, :], full[:, P:, P:]], axis=2).transpose(1, 0, 2)
    return np.concatenate([cos, cos], 1), np.concatenate([-sin, sin], 1), np.ascontiguousarray(decay, dtype=f32)


def slabs(w, order=range(KT)):
    t = w.reshape(KT, P, -1)[list(order)].reshape(SLABS, SLAB_KT, P, -1)
    return t.transpose(0, 2, 1, 3).reshape(SLABS * P, -1)


def kernel(x, norm1_g, w_in, ret_norm_g, q_norm_g, k_norm_g, rel_bias, w_out, norm2_g, w_ff1, w_ff2):
    import concourse.bacc as bacc
    from concourse.bass_utils import run_bass_kernel_spmd as run

    x = np.asarray(x)
    w = np.asarray(w_in)[0].reshape(D_MODEL, 7, HEADS, HD)
    head = lambda first, last, h: w[:, first:last, h, :].reshape(D_MODEL, -1)
    up, down = np.asarray(w_ff1)[0], np.asarray(w_ff2)[0]
    vectors = [np.asarray(v)[0].reshape(-1, P).T for v in (norm1_g, norm2_g, ret_norm_g, q_norm_g, k_norm_g)]
    rel = np.pad(np.asarray(rel_bias)[0], ((0, 0), (P - CHUNK, P - 1)), mode="edge")[:, ::-1]
    windows = np.lib.stride_tricks.sliding_window_view(rel, 2 * P, axis=1)[:, ::-1].transpose(1, 0, 2)
    cos, sin, decay = tables()
    arrays = {
        "x": x,
        "x_cols": x.reshape(SEQ, KT, P).transpose(2, 1, 0),
        "w_att": np.concatenate([slabs(head(4, 7, h)) for h in range(HEADS)]),
        "w_ret": np.concatenate([slabs(head(0, 4, h)) for h in range(HEADS)]),
        "w_out": np.concatenate([slabs(np.asarray(w_out)[0][:, c * N:(c + 1) * N], MIX_ORDER)
                                 for c in range(OUT_GROUPS)]),
        "w_up": np.concatenate([slabs(up[:, c * N:(c + 1) * N]) for c in range(D_FF // N)]),
        "w_down": np.concatenate([slabs(down[g * D_MODEL:(g + 1) * D_MODEL, c * N:(c + 1) * N])
                                  for g in range(FF_ROUNDS) for c in range(D_MODEL // N)]),
        "gains": np.concatenate(vectors, axis=1),
        "rel_windows": windows,
        "rope_cos": cos,
        "rope_sin": sin,
        "decay": decay,
    }
    nc = bacc.Bacc("TRN2", target_bir_lowering=False, num_devices=1)
    arrays = {f"in_{n}": np.ascontiguousarray(a) for n, a in arrays.items()}
    args = [nc.dram_tensor(n, a.shape, mybir.dt.from_np(a.dtype), kind="ExternalInput").ap()
            for n, a in arrays.items()]
    args.append(nc.dram_tensor("out", x.shape, mybir.dt.from_np(x.dtype), kind="ExternalOutput").ap())
    hybrid_block(nc, *args)
    return run(nc, [arrays], core_ids=[0]).results[0]["out"]
```
